# Optimizing a Trainium2 kernel written in Bass

```python
import math
import jax, jax.numpy as jnp
from jax import lax
import numpy as np

D_MODEL = 1024
BATCH = 1
SEQ = 128
DEPTH = 1
DEC_BATCH = 1
DEC_SEQ = 512
PAST_LEN = 128

GRID_W = 64
ROPE_BASE = 10000.0
EPS = 1e-6
NEG_INF = -1e30
Q_BLOCK = 128
A_HEADS = 4
A_HEAD_DIM = 64
A_V_DIM = 2 * A_HEAD_DIM
A_WIDTH = A_HEADS * A_V_DIM
B_HEADS = 8
B_KV_HEADS = 2
B_GROUP = B_HEADS // B_KV_HEADS
B_HEAD_DIM = 64
B_WIDTH = B_HEADS * B_HEAD_DIM
WINDOW = 128
QA_COLS = A_HEADS * 2 * A_HEAD_DIM
KA_COLS = A_HEADS * 2 * A_HEAD_DIM
VA_COLS = A_WIDTH
QB_COLS = B_WIDTH
KB_COLS = B_KV_HEADS * B_HEAD_DIM
VB_COLS = B_KV_HEADS * B_HEAD_DIM
GATE_COLS = 2 * D_MODEL
IN_COLS = QA_COLS + KA_COLS + VA_COLS + QB_COLS + KB_COLS + VB_COLS + GATE_COLS
N_GROUPS = 4
EXPERTS_PER_GROUP = 8
N_EXPERTS = N_GROUPS * EXPERTS_PER_GROUP
TOP_K = 2
D_EXPERT = 512
MOE_BLOCK = 128

kernel_name = "hybrid_diffattn_swa_hmoe_dit_step"

def rms_norm(x, g):
    xf = x.astype(jnp.float32)
    y = xf * lax.rsqrt(jnp.mean(jnp.square(xf), axis=-1, keepdims=True) + EPS)
    return (y * g.astype(jnp.float32)).astype(x.dtype)

def adaln(cvec, w_ada, b_ada):
    m = (jax.nn.silu(cvec) @ w_ada + b_ada)[..., None, :]
    return jnp.split(m, 6, axis=-1)

def axial_rope(n_tok, head_dim):
    n_rows = n_tok // GRID_W
    rows = jnp.repeat(jnp.arange(n_rows), GRID_W).astype(jnp.float32)
    cols = jnp.tile(jnp.arange(GRID_W), n_rows).astype(jnp.float32)
    quarter = head_dim // 4
    inv = ROPE_BASE ** (-jnp.arange(quarter, dtype=jnp.float32) / quarter)
    ang = jnp.concatenate([rows[:, None] * inv, cols[:, None] * inv], axis=-1)
    return jnp.cos(ang), jnp.sin(ang)

def apply_rope(x, cos, sin):
    half = x.shape[-1] // 2
    shape = (x.shape[1],) + (1,) * (x.ndim - 3) + (half,)
    c, s = cos.reshape(shape), sin.reshape(shape)
    xf = x.astype(jnp.float32)
    x1, x2 = xf[..., :half], xf[..., half:]
    return jnp.concatenate([x1 * c - x2 * s, x2 * c + x1 * s], axis=-1).astype(x.dtype)

def sweep_query_blocks(fn, q):
    b, s = q.shape[:2]
    nb = s // Q_BLOCK
    qb = jnp.moveaxis(q.reshape((b, nb, Q_BLOCK) + q.shape[2:]), 1, 0)
    out = lax.map(lambda a: fn(a[0], a[1]), (jnp.arange(nb), qb))
    return jnp.moveaxis(out, 0, 1).reshape((b, s) + out.shape[3:])

def diff_lambda(lq1, lk1, lq2, lk2, lambda_init):
    f = jnp.float32
    return (jnp.exp(jnp.sum(lq1.astype(f) * lk1.astype(f)))
            - jnp.exp(jnp.sum(lq2.astype(f) * lk2.astype(f))) + lambda_init)

def diff_attention(q, k, v, lam, g_head, lambda_init):
    scale = A_HEAD_DIM ** -0.5

    def blk(i, qb):
        s = jnp.einsum('bqhmd,bkhmd->bhmqk', qb, k).astype(jnp.float32) * scale
        p = jax.nn.softmax(s, axis=-1)
        a = p[:, :, 0] - lam * p[:, :, 1]
        return jnp.einsum('bhqk,bkhe->bqhe', a.astype(v.dtype), v)

    o = sweep_query_blocks(blk, q)
    o = rms_norm(o, g_head) * (1.0 - lambda_init)
    return o.reshape(o.shape[:2] + (A_WIDTH,))

def sink_attend(qb, k, v, sink, mask):
    s = jnp.einsum('bqngd,bknd->bngqk', qb, k).astype(jnp.float32) * (B_HEAD_DIM ** -0.5)
    if mask is not None:
        s = jnp.where(mask, s, NEG_INF)
    sk = jnp.broadcast_to(sink.astype(jnp.float32)[None, :, :, None, None], s.shape[:-1] + (1,))
    p = jax.nn.softmax(jnp.concatenate([s, sk], axis=-1), axis=-1)[..., :-1]
    return jnp.einsum('bngqk,bknd->bqngd', p.astype(v.dtype), v)

def swa_context(q, k, v, sink):
    o = sweep_query_blocks(lambda i, qb: sink_attend(qb, k, v, sink, None), q)
    return o.reshape(o.shape[:2] + (B_WIDTH,))

def swa_latent(q, k, v, k_ctx, v_ctx, sink):
    s_len = q.shape[1]
    pad = ((0, 0), (WINDOW, WINDOW), (0, 0), (0, 0))
    kp, vp = jnp.pad(k, pad), jnp.pad(v, pad)
    span = Q_BLOCK + 2 * WINDOW
    rel = jnp.arange(span) - WINDOW
    near = jnp.abs(rel[None, :] - jnp.arange(Q_BLOCK)[:, None]) <= WINDOW
    ctx_vis = jnp.ones((Q_BLOCK, k_ctx.shape[1]), dtype=bool)

    def blk(i, qb):
        start = i * Q_BLOCK
        kb = lax.dynamic_slice_in_dim(kp, start, span, axis=1)
        vb = lax.dynamic_slice_in_dim(vp, start, span, axis=1)
        kabs = start + rel
        band = near & ((kabs >= 0) & (kabs < s_len))[None, :]
        return sink_attend(qb, jnp.concatenate([k_ctx, kb], axis=1), jnp.concatenate([v_ctx, vb], axis=1),
                           sink, jnp.concatenate([ctx_vis, band], axis=1))

    o = sweep_query_blocks(blk, q)
    return o.reshape(o.shape[:2] + (B_WIDTH,))

def split_projection(h, w_in):
    b, s = h.shape[:2]
    z = h @ w_in
    sizes = (QA_COLS, KA_COLS, VA_COLS, QB_COLS, KB_COLS, VB_COLS, D_MODEL, D_MODEL)
    qa, ka, va, qb, kb, vb, ga, gb = jnp.split(z, np.cumsum(sizes)[:-1].tolist(), axis=-1)
    qa = qa.reshape(b, s, A_HEADS, 2, A_HEAD_DIM)
    ka = ka.reshape(b, s, A_HEADS, 2, A_HEAD_DIM)
    va = va.reshape(b, s, A_HEADS, A_V_DIM)
    qb = qb.reshape(b, s, B_KV_HEADS, B_GROUP, B_HEAD_DIM)
    kb = kb.reshape(b, s, B_KV_HEADS, B_HEAD_DIM)
    vb = vb.reshape(b, s, B_KV_HEADS, B_HEAD_DIM)
    return qa, ka, va, qb, kb, vb, ga, gb

def merge_branches(oa, ob, ga, gb, p):
    mix = jax.nn.sigmoid(ga) * (oa @ p['w_proj_a']) + jax.nn.sigmoid(gb) * (ob @ p['w_proj_b'])
    return mix @ p['w_out']

def routed_experts(t, e_id, w_pair, w1, w3, w2):
    n_tok = t.shape[0]
    n_asg = n_tok * TOP_K
    eid = e_id.reshape(n_asg)
    tok = jnp.repeat(jnp.arange(n_tok, dtype=jnp.int32), TOP_K)
    wts = w_pair.reshape(n_asg)
    order = jnp.argsort(eid)
    eid_s, tok_s, w_s = eid[order], tok[order], wts[order]
    counts = jnp.bincount(eid, length=N_EXPERTS)
    padded = (counts + MOE_BLOCK - 1) // MOE_BLOCK * MOE_BLOCK
    pad_end = jnp.cumsum(padded)
    pad_start = pad_end - padded
    start = jnp.cumsum(counts) - counts
    dest = pad_start[eid_s] + jnp.arange(n_asg) - start[eid_s]
    n_blocks = -(-n_asg // MOE_BLOCK) + N_EXPERTS
    buf_tok = jnp.zeros((n_blocks * MOE_BLOCK,), jnp.int32).at[dest].set(tok_s)
    buf_w = jnp.zeros((n_blocks * MOE_BLOCK,), t.dtype).at[dest].set(w_s.astype(t.dtype))
    blk_expert = jnp.minimum(jnp.searchsorted(pad_end, jnp.arange(n_blocks) * MOE_BLOCK, side='right'), N_EXPERTS - 1)

    def blk(args):
        tok_b, w_b, e = args
        xb = t[tok_b]
        hb = jax.nn.silu(xb @ w1[e]) * (xb @ w3[e])
        return (hb @ w2[e]) * w_b[:, None]

    y = lax.map(blk, (buf_tok.reshape(n_blocks, MOE_BLOCK), buf_w.reshape(n_blocks, MOE_BLOCK), blk_expert))
    return jnp.zeros_like(t).at[buf_tok].add(y.reshape(-1, t.shape[1]))

def hierarchical_moe(h, p):
    b, s, d = h.shape
    n_tok = b * s
    t = h.reshape(n_tok, d)
    ar = jnp.arange(n_tok)
    lg = (t @ p['w_router_group'] + p['b_router_group']).astype(jnp.float32)
    g_sel = jnp.argmax(lg, axis=-1)
    g_w = jax.nn.softmax(lg, axis=-1)[ar, g_sel][:, None]
    le = (t @ p['w_router_expert'] + p['b_router_expert']).astype(jnp.float32)
    le_sel = le.reshape(n_tok, N_GROUPS, EXPERTS_PER_GROUP)[ar, g_sel]
    top_v, top_i = lax.top_k(le_sel, TOP_K)
    w_pair = g_w * jax.nn.softmax(top_v, axis=-1)
    e_id = g_sel[:, None] * EXPERTS_PER_GROUP + top_i
    y = routed_experts(t, e_id, w_pair, p['w_e1'], p['w_e3'], p['w_e2'])
    return y.reshape(b, s, d)

def channel_sublayer(x, sh, sc, gt, p):
    h = rms_norm(x, p['g_pre_ffn']) * (1 + sc) + sh
    return x + gt * rms_norm(hierarchical_moe(h, p), p['g_post_ffn'])

def context_layer(x, mod, p, lambda_init):
    sh1, sc1, g1, sh2, sc2, g2 = mod
    h = rms_norm(x, p['g_pre_mix']) * (1 + sc1) + sh1
    qa, ka, va, qb, kb, vb, ga, gb = split_projection(h, p['w_in'])
    lam = diff_lambda(p['lam_q1'], p['lam_k1'], p['lam_q2'], p['lam_k2'], lambda_init)
    oa = diff_attention(qa, ka, va, lam, p['g_diff_head'], lambda_init)
    ob = swa_context(qb, kb, vb, p['sink'].reshape(B_KV_HEADS, B_GROUP))
    x = x + g1 * rms_norm(merge_branches(oa, ob, ga, gb, p), p['g_post_mix'])
    x = channel_sublayer(x, sh2, sc2, g2, p)
    return x, (ka, va, kb, vb)

def latent_layer(x, mod, ctx_kv, rope_a, rope_b, p, lambda_init):
    sh1, sc1, g1, sh2, sc2, g2 = mod
    ka_c, va_c, kb_c, vb_c = ctx_kv
    h = rms_norm(x, p['g_pre_mix']) * (1 + sc1) + sh1
    qa, ka, va, qb, kb, vb, ga, gb = split_projection(h, p['w_in'])
    qa, ka = apply_rope(qa, *rope_a), apply_rope(ka, *rope_a)
    qb, kb = apply_rope(qb, *rope_b), apply_rope(kb, *rope_b)
    lam = diff_lambda(p['lam_q1'], p['lam_k1'], p['lam_q2'], p['lam_k2'], lambda_init)
    oa = diff_attention(qa, jnp.concatenate([ka_c, ka], axis=1), jnp.concatenate([va_c, va], axis=1),
                        lam, p['g_diff_head'], lambda_init)
    ob = swa_latent(qb, kb, vb, kb_c, vb_c, p['sink'].reshape(B_KV_HEADS, B_GROUP))
    x = x + g1 * rms_norm(merge_branches(oa, ob, ga, gb, p), p['g_post_mix'])
    return channel_sublayer(x, sh2, sc2, g2, p)

def setup_inputs(seed: int = 0) -> dict:
    key = jax.random.key(seed)
    ks = iter(jax.random.split(key, 40))
    f = jnp.float32

    def nrm(shape, scale=1.0):
        return jax.random.normal(next(ks), shape, f) * scale

    def gain(shape):
        return 1.0 + nrm(shape, 0.05)

    D = D_MODEL
    return {
        'x_prompt': nrm((BATCH, SEQ, D)),
        'x_sample': nrm((DEC_BATCH, DEC_SEQ, D)),
        'c': nrm((DEC_BATCH, D)),
        'cache_diff_k': nrm((DEC_BATCH, DEPTH, PAST_LEN, A_HEADS, 2, A_HEAD_DIM)),
        'cache_diff_v': nrm((DEC_BATCH, DEPTH, PAST_LEN, A_HEADS, A_V_DIM)),
        'cache_swa_k': nrm((DEC_BATCH, DEPTH, PAST_LEN, B_KV_HEADS, B_HEAD_DIM)),
        'cache_swa_v': nrm((DEC_BATCH, DEPTH, PAST_LEN, B_KV_HEADS, B_HEAD_DIM)),
        'c_ctx': nrm((D,)),
        'w_ada': nrm((DEPTH, D, 6 * D), 0.5 * D ** -0.5),
        'b_ada': nrm((DEPTH, 6 * D), 0.01),
        'g_pre_mix': gain((DEPTH, D)),
        'g_post_mix': gain((DEPTH, D)),
        'g_pre_ffn': gain((DEPTH, D)),
        'g_post_ffn': gain((DEPTH, D)),
        'w_in': nrm((DEPTH, D, IN_COLS), D ** -0.5),
        'lam_q1': nrm((DEPTH, A_HEAD_DIM), 0.1),
        'lam_k1': nrm((DEPTH, A_HEAD_DIM), 0.1),
        'lam_q2': nrm((DEPTH, A_HEAD_DIM), 0.1),
        'lam_k2': nrm((DEPTH, A_HEAD_DIM), 0.1),
        'g_diff_head': gain((DEPTH, A_V_DIM)),
        'sink': nrm((DEPTH, B_HEADS), 0.5),
        'w_proj_a': nrm((DEPTH, A_WIDTH, D), A_WIDTH ** -0.5),
        'w_proj_b': nrm((DEPTH, B_WIDTH, D), B_WIDTH ** -0.5),
        'w_out': nrm((DEPTH, D, D), D ** -0.5),
        'w_router_group': nrm((DEPTH, D, N_GROUPS), D ** -0.5),
        'b_router_group': nrm((DEPTH, N_GROUPS), 0.01),
        'w_router_expert': nrm((DEPTH, D, N_EXPERTS), D ** -0.5),
        'b_router_expert': nrm((DEPTH, N_EXPERTS), 0.01),
        'w_e1': nrm((DEPTH, N_EXPERTS, D, D_EXPERT), D ** -0.5),
        'w_e3': nrm((DEPTH, N_EXPERTS, D, D_EXPERT), D ** -0.5),
        'w_e2': nrm((DEPTH, N_EXPERTS, D_EXPERT, D), D_EXPERT ** -0.5),
    }

def reference(x_prompt, x_sample, c, cache_diff_k, cache_diff_v, cache_swa_k, cache_swa_v, c_ctx,
              w_ada, b_ada, g_pre_mix, g_post_mix, g_pre_ffn, g_post_ffn, w_in,
              lam_q1, lam_k1, lam_q2, lam_k2, g_diff_head, sink, w_proj_a, w_proj_b, w_out,
              w_router_group, b_router_group, w_router_expert, b_router_expert, w_e1, w_e3, w_e2):
    n_lat = x_sample.shape[1]
    rope_a = axial_rope(n_lat, A_HEAD_DIM)
    rope_b = axial_rope(n_lat, B_HEAD_DIM)
    y_p, y_s = x_prompt, x_sample
    ka_l, va_l, kb_l, vb_l = [], [], [], []
    for l in range(DEPTH):
        p = {
            'g_pre_mix': g_pre_mix[l], 'g_post_mix': g_post_mix[l], 'g_pre_ffn': g_pre_ffn[l],
            'g_post_ffn': g_post_ffn[l], 'w_in': w_in[l], 'lam_q1': lam_q1[l], 'lam_k1': lam_k1[l],
            'lam_q2': lam_q2[l], 'lam_k2': lam_k2[l], 'g_diff_head': g_diff_head[l], 'sink': sink[l],
            'w_proj_a': w_proj_a[l], 'w_proj_b': w_proj_b[l], 'w_out': w_out[l],
            'w_router_group': w_router_group[l], 'b_router_group': b_router_group[l],
            'w_router_expert': w_router_expert[l], 'b_router_expert': b_router_expert[l],
            'w_e1': w_e1[l], 'w_e3': w_e3[l], 'w_e2': w_e2[l],
        }
        lambda_init = 0.8 - 0.6 * math.exp(-0.3 * l)
        mod_ctx = adaln(c_ctx, w_ada[l], b_ada[l])
        mod_lat = adaln(c, w_ada[l], b_ada[l])
        y_p, (ka, va, kb, vb) = context_layer(y_p, mod_ctx, p, lambda_init)
        ka_l.append(ka)
        va_l.append(va)
        kb_l.append(kb)
        vb_l.append(vb)
        ctx_kv = (cache_diff_k[:, l], cache_diff_v[:, l], cache_swa_k[:, l], cache_swa_v[:, l])
        y_s = latent_layer(y_s, mod_lat, ctx_kv, rope_a, rope_b, p, lambda_init)
    new_diff_k = jnp.stack(ka_l, axis=1)
    new_diff_v = jnp.stack(va_l, axis=1)
    new_swa_k = jnp.stack(kb_l, axis=1)
    new_swa_v = jnp.stack(vb_l, axis=1)
    return (y_p, y_s, new_diff_k, new_diff_v, new_swa_k, new_swa_v)


_drawn_inputs = setup_inputs


def setup_inputs(seed=0):
    import zlib

    import numpy as np

    out = dict(_drawn_inputs(seed))
    spreads = {}
    factors = {'g_post_ffn': 3.918, 'lam_k2': 2.694, 'sink': 8.0, 'b_router_expert': 3.017}
    for name, (base, spread) in spreads.items():
        noise = np.random.default_rng([zlib.crc32(name.encode()), seed]).standard_normal(out[name].shape)
        drawn = base * np.exp(spread * noise) if base else spread * noise
        out[name] = __import__('jax').numpy.asarray(drawn.astype(out[name].dtype))
    for name, factor in factors.items():
        out[name] = (out[name] * factor).astype(out[name].dtype)
    return out
```

```python
from contextlib import ExitStack

import numpy as np

import concourse.bass as bass
from concourse import mybir

ALU = mybir.AluOpType
ACT = mybir.ActivationFunctionType
F32 = mybir.dt.float32
F32R = mybir.dt.float32r
BF16 = mybir.dt.bfloat16
I32 = mybir.dt.int32
U32 = mybir.dt.uint32
AX = mybir.AxisListType

P = 128
D = 1024
KD = D // P
CTX, LAT, PAST = 128, 512, 128
TOK = CTX + LAT
NT = TOK // P
NLT = LAT // P
AH, HD, AV = 4, 64, 128
BH, BKV, BG = 8, 2, 4
QA, KA, VA, QB, KVB, GA = 0, 512, 1024, 1536, 2048, 2304
IN_COLS = GA + 2 * D
NG, EPG, NE, FE = 4, 8, 32, 512
NR = NG + NE
ROUNDS = TOK // P
UNIT = 4 * 512
NEG = -1e30
EPS = 1e-6
LAMBDA_INIT = 0.2
SCALE = HD ** -0.5
NKT = 6
RAW_MIX, RAW_MOE, HL = 3, 6, 3


def schedule():
    units = [("ada", c, u) for c in range(4) for u in range(2)]
    for c in range(9):
        units += [("in", c, u) for u in range(2)]
        if c < 8:
            units += [("ada", 4 + c, u) for u in range(2)]
    units += [("pa", 0, 0), ("pb", 0, 0), ("pa", 1, 0), ("pb", 1, 0)]
    units += [("out", n, u) for n in range(2) for u in range(2)]
    split_no, n = {}, 0
    for i, (kind, _, _) in enumerate(units):
        if kind != "ada":
            split_no[i] = n
            n += 1
    return units, split_no


def attention_steps():
    steps = [("diff", 0, h, [(0, 1)], 1, [1], 0) for h in range(AH)]
    steps += [("swa", 0, g, [(0, 1)], 1, [1], 1) for g in range(BG)]
    for t in range(1, NT):
        steps += [("diff", t, h, [(P, 5)], 5, [0, 2, 3, 4, 5], 1 + t) for h in range(AH)]
    for t in range(1, NT):
        i = t - 1
        lo, hi = max(0, i - 1), min(NLT - 1, i + 1)
        n = hi - lo + 1
        for g in range(BG):
            steps.append(("swa", t, g, [(P, 1), (2 * P + lo * P, n)], 1 + n, [0] + [2 + j for j in range(lo, hi + 1)], 5 + t))
    return steps


def build(nc, t):
    units, split_no = schedule()
    NU, NS = len(units), len(split_no)
    unit_of_split = {s: i for i, s in split_no.items()}
    steps = attention_steps()
    NSTEP = len(steps)
    NOUT = 2 * NT
    last_step = {q: max(i for i, s in enumerate(steps) if s[6] == q) for q in range(NOUT)}

    with ExitStack() as ctx:
        def sem(name):
            return ctx.enter_context(nc.semaphore(name))

        base = (nc.sbuf_base + 31) // 32 * 32
        place = [base]

        def at(name, cols, dt=F32, offset=None):
            size = cols * (2 if dt == BF16 else 4)
            where = place[0] if offset is None else offset
            if offset is None:
                place[0] += (size + 31) // 32 * 32
                assert place[0] <= nc.sbuf_usable_end, (name, place[0])
            return nc.alloc_sbuf_tensor_at(name, [P, cols], dt, offset=where)

        raw_mix = at("raw_mix", RAW_MIX * UNIT)
        hi = at("w_hi", HL * UNIT, F32R)
        lo = at("w_lo", HL * UNIT, F32R)
        act_hi = at("act_hi", KD * TOK, F32R)
        act_lo = at("act_lo", KD * TOK, F32R)
        rows = at("rows", NT * D)
        att_base = place[0]
        qaT = at("qaT", AH * TOK)
        kaT = at("kaT", AH * NKT * P)
        qbT = at("qbT", BG * TOK)
        kbT = at("kbT", NKT * P)
        va = at("va", NKT * 512)
        vb = at("vb", NKT * P)
        att_end = place[0]
        yrow = at("yrow", NT * D, offset=att_base)
        brow = at("brow", 6 * D, offset=att_base + NT * D * 4)
        h2T = at("h2T", D, offset=att_base + (NT + 6) * D * 4)
        assert att_base + (NT + 7) * D * 4 <= att_end
        scratch = at("scratch", 2 * D, offset=att_base)
        hf = at("hf", 2 * TOK, offset=att_base + 2 * D * 4)
        vecs = at("vecs", P, offset=att_base + (2 * D + 2 * TOK) * 4)
        raw_extra = at("raw_extra", (RAW_MOE - RAW_MIX) * UNIT, offset=att_base)
        xg = at("xg", 2 * D, offset=att_base + 3 * UNIT * 4)
        gsil = at("gsil", FE, offset=att_base + 3 * UNIT * 4 + 2 * D * 4)
        gprod = at("gprod", FE, offset=att_base + 3 * UNIT * 4 + 2 * D * 4 + FE * 4)
        ysb = at("ysb", 2 * D, offset=att_base + 3 * UNIT * 4 + 2 * D * 4 + FE * 8)
        assert 3 * UNIT + 2 * D + 2 * FE + 2 * D <= (NT + 7) * D
        cosin = at("cosin", NLT * 2 * HD)
        pt = at("pt", 2 * 8 * P)
        ident = at("ident", P)
        ones_row = at("ones_row", P)
        maskL = at("maskL", P, BF16)
        maskR = at("maskR", P, BF16)
        ident16 = at("ident16", P, BF16)
        upper16 = at("upper16", P, BF16)
        ones16 = at("ones16", P, BF16)
        vT = at("vT", P)
        cs = at("cs", 2 * KD)
        modc = at("modc", 48 * 2)
        modx = at("modx", 2 * KD * 2)
        modr = at("modr", 4 * 2 * KD)
        stat = at("stat", 64)
        half = at("half", 8)
        lam = at("lam", 4 * HD)
        lamv = at("lamv", 8)
        gh = at("gh", 1)
        sinkb = at("sinkb", BH)
        nsink = at("nsink", BH)
        wr = at("wr", KD * NR)
        br = at("br", NR)
        cidx = at("cidx", P)
        soft = at("soft", 2 * 16)
        orow = at("orow", 512)
        osq = at("osq", 512)
        zs = rows[:, 0:NT * 512].rearrange("p (t n) -> p t n", t=NT)
        zr = rows[:, NT * 512:].rearrange("p (t n) -> p t n", t=NT)
        rt = pt[:, 0:1024].rearrange("p (b n) -> p b n", b=2)
        ex = rows[:, 0:2 * 1280].rearrange("p (b n) -> p b n", b=2)
        ax = rows[:, 2560:2560 + 1280].rearrange("p (b n) -> p b n", b=2)
        of = rows[:, 3840:3840 + 512]
        gst = pt[:, 0:1024].rearrange("p (b n) -> p b n", b=2)
        mtmp = osq[:, :]
        xrow = rows[:, :].rearrange("p (t n) -> p t n", t=NT)
        yr = yrow[:, :].rearrange("p (t n) -> p t n", t=NT)
        ah = act_hi[:, :].rearrange("p (k n) -> p k n", k=KD)
        al = act_lo[:, :].rearrange("p (k n) -> p k n", k=KD)
        qa_v = qaT[:, :].rearrange("p (h n) -> p h n", h=AH)
        ka_v = kaT[:, :].rearrange("p (h n) -> p h n", h=AH)
        qb_v = qbT[:, :].rearrange("p (h n) -> p h n", h=BG)
        va_v = va[:, :].rearrange("p (t n) -> p t n", t=NKT)
        vb_v = vb[:, :].rearrange("p (t n) -> p t n", t=NKT)
        cs_v = cosin[:, :].rearrange("p (t s n) -> p t s n", t=NLT, s=2)
        br_v = brow[:, :].rearrange("p (r n) -> p r n", r=6)
        wr_v = wr[:, :].rearrange("p (k n) -> p k n", k=KD)

        wk = at("pair_weights", 2 * NT)
        tab_s = at("scatter_rows", ROUNDS * NE, U32)
        tab_g = at("gather_rows", ROUNDS * NE, U32)
        cnt_i = at("largest_count", 1, I32)
        idx_g = at("gather_column", 2, U32)
        idx_s = at("scatter_column", 2, U32)
        rbase = [att_base + (NT + 2) * D * 4]

        def rb(name, cols, dt=F32):
            a = at(name, cols, dt, offset=rbase[0])
            rbase[0] += (cols * (2 if dt == BF16 else 4) + 31) // 32 * 32
            assert rbase[0] <= att_base + (NT + 6) * D * 4
            return a

        rL = rb("router_logits", NT * NR)
        rle = rb("masked_logits", NT * NE)
        rt1 = rb("route_tmp1", NT * NE)
        rt2 = rb("route_tmp2", NT * NE)
        oh = [rb(f"onehot{k}", NT * NE) for k in range(2)]
        m16 = rb("assigned16", NT * NE, BF16)
        rpre = rb("positions", NT * NE)
        rex = rb("exponents", NT * 5)
        rsm = rb("route_small", 16 * NT)
        rposk = rb("pos_k", 2 * NT)
        rround = rb("round_k", 2 * NT)
        rrhs = [rb(f"slot_values{k}", NT * ROUNDS * NE) for k in range(2)]
        roc = rb("slot_onehot", 2 * P)
        iota32 = at("iota32", NE)
        rr = at("window_norms", 16)
        ci_i = at("column_index", P, I32, offset=att_base)
        tv_i = at("token_value", 2 * NT, I32, offset=att_base + P * 4)
        kcache = at("cached_keys", 640, offset=att_base + (2 * D + 2 * TOK + P) * 4)
        tokval = at("tokval", 2 * NT)

        def raw(slot):
            if slot < RAW_MIX:
                return raw_mix[:, slot * UNIT:(slot + 1) * UNIT].rearrange("p (k n) -> p k n", k=4)
            s = slot - RAW_MIX
            return raw_extra[:, s * UNIT:(s + 1) * UNIT].rearrange("p (k n) -> p k n", k=4)

        def whi(slot):
            return hi[:, slot * UNIT:(slot + 1) * UNIT].rearrange("p (k n) -> p k n", k=4)

        def wlo(slot):
            return lo[:, slot * UNIT:(slot + 1) * UNIT].rearrange("p (k n) -> p k n", k=4)

        psum = ctx.enter_context(nc.psum_tensor("psum", [P, 8 * 512], F32))

        def bank(b, n=1):
            return psum[:, b * 512:(b + n) * 512]

        gates_d = nc.dram_tensor("gates_scratch", (TOK, 2 * D), F32).ap()
        h2_d = nc.dram_tensor("h2_scratch", (TOK, D), F32).ap()
        y_d = nc.dram_tensor("y_scratch", (2 * TOK, D), F32).ap()
        w_ada = t["w_ada"][0].rearrange("(k p) n -> p k n", p=P)
        w_in = t["w_in"][0].rearrange("(k p) n -> p k n", p=P)
        w_pa = t["w_proj_a"][0].rearrange("(k p) n -> p k n", p=P)
        w_pb = t["w_proj_b"][0].rearrange("(k p) n -> p k n", p=P)
        w_out = t["w_out"][0].rearrange("(k p) n -> p k n", p=P)
        w1 = t["w_e1"].rearrange("l e (k p) n -> (l e) p k n", p=P)
        w3 = t["w_e3"].rearrange("l e (k p) n -> (l e) p k n", p=P)
        w2 = t["w_e2"].rearrange("l e (k p) n -> (l e) p k n", p=P)
        x_src = [t["x_prompt"][0]] + [t["x_sample"][0, i * P:(i + 1) * P] for i in range(NLT)]
        y_dst = [t["y_prompt"][0]] + [t["y_sample"][0, i * P:(i + 1) * P] for i in range(NLT)]
        new_ka = t["new_diff_k"][0, 0].rearrange("s h m d -> s (h m d)")
        new_va = t["new_diff_v"][0, 0].rearrange("s h e -> s (h e)")
        new_kb = t["new_swa_k"][0, 0].rearrange("s h d -> s (h d)")
        new_vb = t["new_swa_v"][0, 0].rearrange("s h d -> s (h d)")

        def unit_src(i):
            kind, c, u = units[i]
            w = 256 if (kind, c) == ("in", 4) else 512
            col = {"in": [QA, KA, VA, QB, KVB] + [GA + 512 * j for j in range(4)]}.get(kind, [512 * j for j in range(12)])[c]
            m = {"ada": w_ada, "in": w_in, "pa": w_pa, "pb": w_pb, "out": w_out}[kind]
            return m[:, 4 * u:4 * u + 4, col:col + w], w

        small_in = sem("small_inputs_landed")
        x_in = [sem(f"x_tile{i}_landed") for i in range(NT)]
        const_made = sem("constants_made")
        raw_in = [sem(f"raw_slot{i}_landed") for i in range(RAW_MOE)]
        hi_done = sem("weight_hi_done")
        lo_done = sem("weight_lo_done")
        tile_mm = sem("tile_products_done")
        v_tr = sem("vectors_transposed")
        v_cp = sem("vectors_copied")
        cs_done = sem("silu_c_done")
        ada_mm = sem("ada_chunk_done")
        mod_done = sem("modulation_columns_done")
        sq_done = sem("x_squares_done")
        rstd_done = sem("x_rstd_done")
        xn_done = sem("x_normed")
        xt_done = sem("x_slice_transposed")
        hf_done = sem("h_slice_done")
        hh_done = sem("h_hi_done")
        hl_done = sem("h_lo_done")
        kc_tr = sem("cache_keys_transposed")
        kc_cp = sem("cache_keys_copied")
        cache_in = sem("cache_landed")
        acc_free = sem("accumulator_evacuated")
        rope_a = sem("rope_cos_part_done")
        rope_b = sem("rope_sin_part_done")
        rope_done = sem("rope_done")
        zt_done = sem("projection_transposed")
        zt_cp = sem("transposed_projection_copied")
        kv_out = sem("new_kv_stored")
        gate_out = [sem(f"gates_tile{i}_stored") for i in range(NT)]
        ve_link = sem("vector_chain")
        po_link = sem("gpsimd_chain")
        ac_link = sem("scalar_chain")
        s_half = sem("first_map_scores_done")
        s_done = sem("scores_done")
        mx_done = sem("score_max_done")
        ex_done = sem("exp_done")
        pa_done = sem("probabilities_ready")
        pt_done = sem("probabilities_transposed")
        pt_dve = sem("transposes_copied_by_vector")
        pt_act = sem("transposes_copied_by_scalar")
        pv_done = sem("values_summed")
        o_cp = sem("attention_output_copied")
        o_ready = sem("attention_rows_ready")
        of_done = sem("attention_columns_copied")
        oh_done = sem("attention_hi_done")
        ol_done = sem("attention_lo_done")
        b_tr = sem("modulation_rows_made")
        b_cp = sem("modulation_rows_copied")
        g_in = [sem(f"gate_slot{i}_landed") for i in range(2)]
        mix_done = sem("mix_part_done")
        mt_done = sem("mix_transposed")
        mh_done = sem("mix_hi_done")
        ml_done = sem("mix_lo_done")
        x2_in = [sem(f"x_tile{i}_landed_again") for i in range(NT)]
        y_cp = sem("merged_rows_copied")
        ysq = sem("merged_squares_done")
        yrs = sem("merged_rstd_done")
        yn = sem("merged_scaled")
        x1_done = sem("x1_done")
        x1sq = sem("x1_squares_done")
        x1rs = sem("x1_rstd_done")
        h2_done = sem("h2_rows_done")
        h2_out = sem("h2_stored")
        h2t_done = sem("h2_transposed")
        h2t_cp = sem("h2_transposed_copied")
        rl_done = sem("router_logits_done")
        r_exp_in = sem("router_exponents_ready")
        r_exp = sem("router_exp_done")
        m_ready = sem("assignments_ready")
        pre_done = sem("positions_counted")
        oc_done = sem("slot_onehot_done")
        tab_mm = sem("slot_table_summed")
        tab_done = sem("slot_tables_ready")
        moe_idx = sem("expert_indices_copied")
        moe_g = [sem(f"expert_rows{i}_gathered") for i in range(2)]
        moe_xt = sem("expert_rows_transposed")
        moe_xh = sem("expert_x_hi_done")
        moe_xl = sem("expert_x_lo_done")
        moe_mm = sem("expert_unit_done")
        moe_si = sem("expert_silu_done")
        moe_gp = sem("expert_product_done")
        moe_gt = sem("expert_product_transposed")
        moe_gh = sem("expert_g_hi_done")
        moe_gl = sem("expert_g_lo_done")
        moe_ya = sem("expert_y_copied_by_scalar")
        moe_yv = sem("expert_y_copied_by_vector")
        moe_sc = [sem(f"expert_y_scattered{i}") for i in range(2)]
        yp_in = [sem(f"y_pair{i}_landed") for i in range(NT)]
        c_sum = sem("pair_summed")
        c_sq = sem("pair_squares_done")
        c_rs = sem("pair_rstd_done")
        c_out = sem("final_rows_ready")
        final_out = sem("final_rows_stored")
        all_scattered = sem("all_expert_rows_stored")
        row_dmas = sem("row_dmas_issued")
        gi_done = sem("gather_column_copied")
        si_done = sem("scatter_column_copied")
        lam_part = sem("lambda_dots_done")
        lam_sum = sem("lambda_inputs_ready")
        lam_exp = sem("lambda_exponentials_done")
        ysum = sem("merged_squares_summed")
        head_sum = sem("head_squares_summed")
        g2_mm = sem("last_gate_rows_made")
        g2_cp = sem("last_gate_rows_copied")
        c_part = sem("pair_parts_done")

        uses = []

        def groups(i):
            kind, _, _, _, nk, _, _ = steps[i]
            n = nk if kind == "diff" else 2 * nk
            return [list(range(a, min(a + 4, n))) for a in range(0, n, 4)]

        flush = {}
        for q in range(NOUT):
            flush.setdefault(min(last_step[q] + 2, NSTEP), []).append(q)
        for i in range(NSTEP):
            for j in range(len(groups(i))):
                uses.append(("p", i, j, "dve" if j == 0 else "act"))
            for q in flush.get(i, []):
                uses.append(("o", q, 0, "dve"))
        for q in flush.get(NSTEP, []):
            uses.append(("o", q, 0, "dve"))
        use_no = {(k, i, j): n for n, (k, i, j, _) in enumerate(uses)}
        made = {n: n + 1 for n in range(len(uses))}
        emptied, count = {}, {"dve": 0, "act": 0}
        for n, (_, _, _, e) in enumerate(uses):
            count[e] += 1
            emptied[n] = (e, count[e])
        N_DVE, N_ACT = count["dve"], count["act"]

        def wait_emptied(eng, n):
            e, v = emptied[n]
            eng.wait_ge(pt_dve if e == "dve" else pt_act, v)

        def s_view(i):
            kind, _, _, _, nk, _, _ = steps[i]
            b, w = 3 * (i % 2), nk * P
            if kind == "diff" and nk > 1:
                return psum[:, b * 512:b * 512 + 2 * w].rearrange("p (m n) -> p m n", m=2)
            return psum[:, b * 512:(b + 2) * 512].rearrange("p (m n) -> p m n", m=2)[:, :, 0:w]

        EXC, total = [], 0
        for st in steps:
            total += 2 if st[0] == "diff" else 3
            EXC.append(total)
        NTR = 4 * NT
        UPR = 6 * NE
        before = [sum(1 for n in range(NU) if n % RAW_MIX == s) for s in range(RAW_MIX)] + [0] * (RAW_MOE - RAW_MIX)

        def raw_pair(i):
            if i < RAW_MIX:
                return raw_mix[:, i * UNIT:(i + 1) * UNIT]
            return raw_extra[:, (i - RAW_MIX) * UNIT:(i - RAW_MIX + 1) * UNIT]

        def out_place(q):
            st = steps[last_step[q]]
            k = 0 if st[0] == "diff" else 4
            return slice(None), slice(k, k + 4), slice(st[1] * P, (st[1] + 1) * P)

        def out_transpose(pe, q):
            n = use_no[("o", q, 0)]
            pe.wait_ge(o_cp, q + 1)
            if steps[last_step[q]][0] == "diff":
                pe.wait_ge(o_ready, 1 + sum(1 for x in range(q) if steps[last_step[x]][0] == "diff"))
            wait_emptied(pe, n - 1)
            for x in range(4):
                ins = pe.transpose(bank(6)[:, x * P:(x + 1) * P], orow[:, x * P:(x + 1) * P], ident[:, :])
            ins.then_inc(pt_done, 1)

        def attention_hi(ac, q):
            ac.wait_ge(pt_dve, emptied[use_no[("o", q, 0)]][1])
            ac.activation(ah[out_place(q)], of.rearrange("p (k n) -> p k n", k=4), ACT.Copy).then_inc(oh_done, 1)

        def attention_lo(ve, q):
            n = use_no[("o", q, 0)]
            ve.wait_ge(pt_done, n + 1)
            if q:
                ve.wait_ge(ol_done, q)
            if steps[last_step[q]][0] == "diff":
                ve.tensor_scalar(of, bank(6), gh[:, 0:1], None, ALU.mult).then_inc(pt_dve, 1)
            else:
                ve.tensor_copy(of, bank(6)).then_inc(pt_dve, 1)
            ve.wait_ge(oh_done, q + 1)
            ve.tensor_tensor(al[out_place(q)], of.rearrange("p (k n) -> p k n", k=4), ah[out_place(q)].bitcast(F32), ALU.subtract).then_inc(ol_done, 1)

        block = ctx.enter_context(nc.Block())

        @block.sync
        def _(sp):
            for i in range(16):
                src = t["c_ctx"] if i < 8 else t["c"][0]
                if i % 8 == 0:
                    sp.dma_start(vecs[i:i + 8, :], src.rearrange("(k p) -> k p", p=P)).then_inc(small_in, 16)
            sp.dma_start(vecs[16:64, :], t["b_ada"][0].rearrange("(k p) -> k p", p=P)).then_inc(small_in, 16)
            for i, name in enumerate(["g_pre_mix", "g_post_mix", "g_pre_ffn", "g_post_ffn"]):
                sp.dma_start(vecs[64 + 8 * i:72 + 8 * i, :], t[name][0].rearrange("(k p) -> k p", p=P)).then_inc(small_in, 16)
            sp.dma_start(vecs[96:97, :], t["g_diff_head"]).then_inc(small_in, 16)
            for i in range(NT):
                sp.dma_start(xrow[:, i, :], x_src[i]).then_inc(x_in[i], 16)
            for n in range(NU):
                if n >= RAW_MIX:
                    kind, c, _ = units[n - RAW_MIX]
                    if kind == "ada":
                        sp.wait_ge(ada_mm, c + 1)
                    else:
                        sp.wait_ge(lo_done, split_no[n - RAW_MIX] + 1)
                src, w = unit_src(n)
                sp.dma_start(raw(n % RAW_MIX)[:, :, 0:w], src).then_inc(raw_in[n % RAW_MIX], 16)

            last = [max(n for n in range(NU) if n % RAW_MIX == s) for s in range(RAW_MIX)]

            def load(src, slot, wait):
                if wait is not None:
                    sp.wait_ge(lo_done, wait)
                sp.dma_start(raw(slot), src).then_inc(raw_in[slot], 16)

            def first(r, e0):
                for j in range(2):
                    if r == 0:
                        load(w1[e0][:, 4 * j:4 * j + 4, :], j, split_no[last[j]] + 1)
                    else:
                        load(w1[e0][:, 4 * j:4 * j + 4, :], j, NS + 6 * NE * r + j - 5)

            def body(r, e, base, nxt):
                srcs = [(w3[e, :, 0:4, :], 2), (w3[e, :, 4:8, :], 3)]
                if nxt is not None:
                    srcs += [(w1[nxt, :, 0:4, :], 4), (w1[nxt, :, 4:8, :], 5)]
                srcs += [(w2[e, :, :, 0:512], (2 + len(srcs)) % 6), (w2[e, :, :, 512:1024], (3 + len(srcs)) % 6)]
                for j, (src, slot) in enumerate(srcs):
                    load(src, slot, base + j)

            def a_round(r):
                s0 = NS + 6 * NE * r
                first(r, 0)
                if r == 0:
                    sp.wait_ge(lo_done, NS)
                    sp.wait_ge(h2_out, 16 * NT)
                    sp.wait_ge(h2t_cp, 2 * NT)
                    sp.wait_ge(rl_done, 1)
                    srcs = [w3[0][:, 0:4, :], w3[0][:, 4:8, :], w1[1][:, 0:4, :], w1[1][:, 4:8, :]]
                    for j, src in enumerate(srcs):
                        load(src, 2 + j, None)
                    load(w2[0][:, :, 0:512], 0, s0 + 1)
                    load(w2[0][:, :, 512:1024], 1, s0 + 2)
                else:
                    body(r, 0, s0 - 3, 1)
                with sp.Fori(1, NE - 1) as e:
                    body(r, e, e * 6 + (s0 - 3), e + 1)
                body(r, NE - 1, s0 - 3 + 6 * (NE - 1), None)

            a_round(0)
            sp.wait_ge(tab_done, 1)
            most = sp.value_load(cnt_i[0:1, 0:1], min_val=0, max_val=TOK)
            for r in range(1, ROUNDS):
                with sp.If(most > P * r):
                    a_round(r)

            sp.wait_ge(all_scattered, 1)
            for i in range(NT):
                sp.dma_start(raw_pair(i), y_d[2 * P * i:2 * P * (i + 1), :].rearrange("(p k) n -> p (k n)", k=2)).then_inc(yp_in[i], 16)
            for i in range(NT):
                sp.wait_ge(c_out, i + 1)
                sp.dma_start(y_dst[i], xrow[:, i, :]).then_inc(final_out, 16)
            sp.wait_ge(final_out, 16 * NT)
            sp.wait_ge(kv_out, 16 * 4)

        @block.gpsimd
        def _(po):
            chain = [0]

            def link(ins):
                chain[0] += 1
                ins.then_inc(po_link, 1)
                po.wait_ge(po_link, chain[0])

            lam_names = ["lam_q1", "lam_k1", "lam_q2", "lam_k2"]
            for i, name in enumerate(lam_names):
                po.dma_start(lam[:, i * HD:(i + 1) * HD], t[name][0].partition_broadcast(P)).then_inc(cache_in, 16)
            po.dma_start(sinkb[:, :], t["sink"][0].partition_broadcast(P)).then_inc(cache_in, 16)
            po.dma_start(br[:, 0:NG], t["b_router_group"][0].partition_broadcast(P)).then_inc(cache_in, 16)
            po.dma_start(br[:, NG:NR], t["b_router_expert"][0].partition_broadcast(P)).then_inc(cache_in, 16)
            po.dma_start(wr_v[:, :, 0:NG], t["w_router_group"][0].rearrange("(k p) n -> p k n", p=P)).then_inc(cache_in, 16)
            po.dma_start(wr_v[:, :, NG:NR], t["w_router_expert"][0].rearrange("(k p) n -> p k n", p=P)).then_inc(cache_in, 16)
            po.dma_start(cosin[:, :], t["rope"]).then_inc(cache_in, 16)
            po.dma_start(kcache[:, 0:512], t["cache_diff_k"][0, 0].rearrange("s h m d -> s (h m d)")).then_inc(cache_in, 16)
            po.dma_start(kcache[:, 512:640], t["cache_swa_k"][0, 0].rearrange("s h d -> s (h d)")).then_inc(cache_in, 16)
            po.dma_start(va_v[:, 0, :], t["cache_diff_v"][0, 0].rearrange("s h e -> s (h e)")).then_inc(cache_in, 16)
            po.dma_start(vb_v[:, 0, :], t["cache_swa_v"][0, 0].rearrange("s h d -> s (h d)")).then_inc(cache_in, 16)

            link(po.memset(ident[:, :], 0.0))
            link(po.affine_select(out=ident[:, :], in_=ident[:, :], compare_op=ALU.not_equal, fill=1.0, base=0,
                                  pattern=[[-1, P]], channel_multiplier=1))
            link(po.tensor_copy(ident16[:, :], ident[:, :]))
            link(po.memset(ones16[:, :], 1.0))
            link(po.memset(half[:, :], -0.5))
            link(po.memset(maskL[:, :], 0.0))
            link(po.memset(maskR[:, :], 0.0))
            link(po.affine_select(out=maskL[:, :], in_=maskL[:, :], compare_op=ALU.is_ge, fill=NEG, base=0,
                                  pattern=[[1, P]], channel_multiplier=-1))
            link(po.affine_select(out=maskR[:, :], in_=maskR[:, :], compare_op=ALU.is_ge, fill=NEG, base=0,
                                  pattern=[[-1, P]], channel_multiplier=1))
            link(po.affine_select(out=upper16[:, :], in_=ones16[:, :], compare_op=ALU.is_gt, fill=0.0, base=0,
                                  pattern=[[1, P]], channel_multiplier=-1))
            link(po.iota(ci_i[:, :], pattern=[[1, P]], base=0, channel_multiplier=0))
            link(po.tensor_copy(cidx[:, :], ci_i[:, :]))
            link(po.tensor_copy(iota32[:, :], ci_i[:, 0:NE]))
            link(po.iota(tv_i[:, :], pattern=[[2 * P, NT], [1, 2]], base=1, channel_multiplier=2))
            po.tensor_copy(tokval[:, :], tv_i[:, :]).then_inc(const_made, 1)

            def rsqrt(out, in_, n, scale):
                link(po.tensor_scalar(out, in_, scale, EPS, ALU.mult, ALU.add))
                return po.tensor_tensor(out, out, half[:, 0:n], ALU.pow)

            po.wait_ge(sq_done, NT)
            rsqrt(stat[:, 8:8 + NT], stat[:, 0:NT], NT, 1.0 / D).then_inc(rstd_done, 1)

            rope_no = 0
            for c in range(9):
                if c == 2:
                    po.wait_ge(acc_free, 5 * c + 1)
                    po.dma_start(new_va, va_v[:, 1, :]).then_inc(kv_out, 16)
                elif c in (1, 4):
                    po.wait_ge(acc_free, 5 * c + 1)
                    if c == 1:
                        po.dma_start(new_ka, zs[:, 0, :]).then_inc(kv_out, 16)
                    else:
                        po.dma_start(new_kb, zs[:, 0, 0:P]).then_inc(kv_out, 16)
                        po.dma_start(new_vb, vb_v[:, 1, :]).then_inc(kv_out, 16)
                if c in (0, 1, 3, 4):
                    for i in range(1, NT):
                        po.wait_ge(acc_free, 5 * c + i + 1)
                        if rope_no >= 2:
                            po.wait_ge(rope_done, (rope_no - 2) // 4 * NT + (rope_no - 2) % 4 + 2)
                        b = rope_no % 2
                        S = cs_v[:, i - 1, 1, :]
                        if c == 3:
                            z = zs[:, i, :].rearrange("p (n g d) -> p n g d", n=2, g=4)
                            o = rt[:, b, :].rearrange("p (g n d) -> p n g d", g=4, n=2)
                            for hf_ in range(2):
                                s = S[:, 32 * hf_:32 * hf_ + 32].unsqueeze(1).broadcast_to([P, 4, 32])
                                for n in range(2):
                                    ins = po.tensor_tensor(o[:, n, :, 32 * hf_:32 * hf_ + 32],
                                                           z[:, n, :, 32 - 32 * hf_:64 - 32 * hf_], s, ALU.mult)
                        else:
                            nh = 2 if c == 4 else 8
                            z = zs[:, i, 0:nh * HD].rearrange("p (h d) -> p h d", h=nh)
                            o = rt[:, b, 0:nh * HD].rearrange("p (h d) -> p h d", h=nh)
                            for hf_ in range(2):
                                s = S[:, 32 * hf_:32 * hf_ + 32].unsqueeze(1).broadcast_to([P, nh, 32])
                                ins = po.tensor_tensor(o[:, :, 32 * hf_:32 * hf_ + 32],
                                                       z[:, :, 32 - 32 * hf_:64 - 32 * hf_], s, ALU.mult)
                        ins.then_inc(rope_b, 1)
                        rope_no += 1
                if c >= 5:
                    for i in range(NT):
                        po.wait_ge(acc_free, 5 * c + i + 1)
                        po.dma_start(gates_d[i * P:(i + 1) * P, (c - 5) * 512:(c - 4) * 512], zs[:, i, :]).then_inc(gate_out[i], 16)

            for q in range(NOUT):
                if steps[last_step[q]][0] != "diff":
                    continue
                po.wait_ge(head_sum, AH * (1 + sum(1 for x in range(q) if steps[last_step[x]][0] == "diff")))
                link(rsqrt(stat[:, 24:28], stat[:, 16:20], AH, 1.0 / AV))
                o3 = orow[:, :].rearrange("p (h e) -> p h e", h=AH)
                po.tensor_tensor(o3, o3, stat[:, 24:28].unsqueeze(2).broadcast_to([P, AH, AV]), ALU.mult).then_inc(o_ready, 1)

            for g in range(4):
                branch, n = g % 2, g // 2
                for i in range(NT):
                    m = 5 * g + i
                    if m == 0:
                        po.wait_ge(pv_done, NSTEP)
                    if g == 0:
                        po.wait_ge(gate_out[i], 64)
                    if m >= 2:
                        po.wait_ge(mix_done, m - 1)
                    po.dma_start(gst[:, m % 2, :], gates_d[i * P:(i + 1) * P, branch * D + n * 512:branch * D + n * 512 + 512]).then_inc(g_in[m % 2], 16)
            for i in range(NT):
                po.wait_ge(mt_done, 2 * i + 2)
                po.dma_start(xrow[:, i, :], x_src[i]).then_inc(x2_in[i], 16)
            po.wait_ge(ysum, 1)
            rsqrt(stat[:, 8:8 + NT], stat[:, 0:NT], NT, 1.0 / D).then_inc(yrs, 1)
            for i in range(NT):
                po.wait_ge(yn, i + 1)
                po.wait_ge(x2_in[i], 16)
                po.tensor_tensor(xrow[:, i, :], xrow[:, i, :], yr[:, i, :], ALU.add).then_inc(x1_done, 1)
            po.wait_ge(x1sq, NT)
            rsqrt(stat[:, 40:40 + NT], stat[:, 32:32 + NT], NT, 1.0 / D).then_inc(x1rs, 1)
            for i in range(NT):
                po.wait_ge(h2_done, i + 1)
                po.dma_start(h2_d[i * P:(i + 1) * P, :], yr[:, i, :]).then_inc(h2_out, 16)

            last_row, last_pair = po.to_reg(TOK - 1), po.to_reg(2 * TOK - 1)
            po.wait_ge(h2_out, 16 * NT)
            po.wait_ge(tab_done, 1)
            link(po.memset(xg[:, :], 0.0))

            def gather(n, after, par):
                n = po.snap(n) if not isinstance(n, int) else n
                if after is not None:
                    po.wait_ge(moe_xt, after)
                po.tensor_copy(idx_g[:, par:par + 1], tab_g[:, bass.ds(n, 1)]).then_inc(gi_done, 1)
                po.wait_ge(gi_done, n + 1)
                po.sem_inc(row_dmas, 1)
                po.indirect_dma_start(out=xg[:, par * D:(par + 1) * D], out_offset=None, in_=h2_d,
                                      in_offset=bass.IndirectOffsetOnAxis(idx_g[:, par:par + 1], 0),
                                      bounds_check=last_row, oob_is_err=False).then_inc(moe_g[par], 16)

            def scatter(n, par, pair):
                n = po.snap(n) if not isinstance(n, int) else n
                po.wait_ge(moe_sc[par], pair * 16)
                po.tensor_copy(idx_s[:, par:par + 1], tab_s[:, bass.ds(n, 1)]).then_inc(si_done, 1)
                po.wait_ge(si_done, n + 1)
                po.wait_ge(moe_ya, n + 1)
                po.wait_ge(moe_yv, n + 1)
                po.sem_inc(row_dmas, 1)
                po.indirect_dma_start(out=y_d, out_offset=bass.IndirectOffsetOnAxis(idx_s[:, par:par + 1], 0),
                                      in_=ysb[:, par * D:(par + 1) * D], in_offset=None,
                                      bounds_check=last_pair, oob_is_err=False).then_inc(moe_sc[par], 16)

            def a_round(r):
                b = NE * r
                gather(b, b if r else None, 0)
                gather(b + 1, b if r else None, 1)
                with po.Fori(0, NE // 2 - 1) as i:
                    for j in range(2):
                        gather(i * 2 + (b + j + 2), i * 2 + (b + j + 1), j)
                        scatter(i * 2 + (b + j), j, i + b // 2)
                scatter(b + NE - 2, 0, (b + NE - 2) // 2)
                scatter(b + NE - 1, 1, (b + NE - 2) // 2)
                for j in range(2):
                    po.wait_ge(moe_sc[j], 16 * (b + NE) // 2)

            a_round(0)
            most = po.value_load(cnt_i[0:1, 0:1], min_val=0, max_val=TOK)
            for r in range(1, ROUNDS):
                with po.If(most > P * r):
                    a_round(r)
            po.sem_inc(all_scattered, 1)

            po.wait_ge(c_sq, NT)
            rsqrt(stat[:, 8:8 + NT], stat[:, 0:NT], NT, 1.0 / D).then_inc(c_rs, 1)

        @block.scalar
        def _(ac):
            chain = [0]

            def link(ins):
                chain[0] += 1
                ins.then_inc(ac_link, 1)
                ac.wait_ge(ac_link, chain[0])

            def split_hi(s):
                n = unit_of_split[s]
                _, w = unit_src(n)
                ac.wait_ge(raw_in[n % RAW_MIX], 16 * (n // RAW_MIX + 1))
                if s >= HL:
                    ac.wait_ge(tile_mm, 5 * (s - HL + 1))
                ac.activation(whi(s % HL)[:, :, 0:w], raw(n % RAW_MIX)[:, :, 0:w], ACT.Copy).then_inc(hi_done, 1)

            ac.wait_ge(v_cp, 1)
            ac.activation(cs[:, :].rearrange("p (k s) -> p k s", s=2), vT[:, 0:16].rearrange("p (s k) -> p k s", s=2), ACT.Silu).then_inc(cs_done, 1)
            for i in range(NT):
                ac.wait_ge(x_in[i], 16)
                if i:
                    ac.wait_ge(sq_done, i)
                ac.activation(scratch[:, 0:D], xrow[:, i, :], ACT.Square, accum_out=stat[:, i:i + 1]).then_inc(sq_done, 1)
            ac.wait_ge(rstd_done, 1)
            for i in range(NT):
                ac.activation(xrow[:, i, :], xrow[:, i, :], ACT.Copy, scale=stat[:, 8 + i:9 + i]).then_inc(xn_done, 1)
            split_hi(0)
            split_hi(1)
            for k in range(KD):
                ac.wait_ge(hf_done, k + 1)
                ac.activation(ah[:, k, :], hf[:, (k % 2) * TOK:(k % 2 + 1) * TOK], ACT.Copy).then_inc(hh_done, 1)
            ac.wait_ge(kc_tr, 1)
            ac.wait_ge(hl_done, KD)
            ac.activation(ka_v[:, :, P:2 * P], bank(5).rearrange("p (h n) -> p h n", h=4), ACT.Copy).then_inc(kc_cp, 1)
            ac.activation(kbT[:, P:2 * P], bank(7)[:, 0:P], ACT.Copy).then_inc(kc_cp, 1)

            tr = 0

            def copy_transposed(c, i):
                nonlocal tr
                b = 5 if tr % 2 == 0 else 7
                ac.wait_ge(zt_done, tr + 1)
                key = P * i + (P if i else 0)
                if c == 4:
                    ac.activation(kbT[:, key:key + P], bank(b)[:, 0:P], ACT.Copy).then_inc(zt_cp, 1)
                else:
                    dst = {0: qa_v[:, :, i * P:(i + 1) * P], 1: ka_v[:, :, key:key + P], 3: qb_v[:, :, i * P:(i + 1) * P]}[c]
                    ac.activation(dst, bank(b).rearrange("p (h n) -> p h n", h=4), ACT.Copy).then_inc(zt_cp, 1)
                tr += 1

            for c in range(9):
                split_hi(2 * c + 2)
                for i in range(NT):
                    if c - 1 in (0, 1, 3, 4):
                        copy_transposed(c - 1, i)
                for i in range(NT):
                    ac.wait_ge(tile_mm, 5 * (2 * c + 1) + i + 1)
                    if c in (1, 3, 4, 5):
                        ac.wait_ge(rope_done, NT * {1: 0, 3: 1, 4: 2, 5: 3}[c] + i + 1)
                        if i == 0 and c in (3, 5):
                            ac.wait_ge(kv_out, {3: 32, 5: 64}[c])
                    if c > 5:
                        ac.wait_ge(gate_out[i], 16 * (c - 5))
                    if c == 2:
                        ac.activation(va_v[:, 1 + i, :], bank(i), ACT.Copy).then_inc(acc_free, 1)
                    elif c == 4:
                        link(ac.activation(zs[:, i, 0:P], bank(i)[:, 0:P], ACT.Copy))
                        ac.activation(vb_v[:, 1 + i, :], bank(i)[:, P:2 * P], ACT.Copy).then_inc(acc_free, 1)
                    elif c >= 5:
                        ac.activation(zs[:, i, :], bank(i), ACT.Sigmoid).then_inc(acc_free, 1)
                    else:
                        ac.activation(zs[:, i, :], bank(i), ACT.Copy).then_inc(acc_free, 1)
                split_hi(2 * c + 3)

            ac.wait_ge(lam_sum, 1)
            ac.activation(lamv[:, 2:4], lamv[:, 0:2], ACT.Exp).then_inc(lam_exp, 1)

            def exponentials(i):
                kind, b, w = steps[i][0], i % 2, steps[i][4] * P
                ac.wait_ge(mx_done, i + 1)
                if i < 2:
                    for g in gate_out:
                        ac.wait_ge(g, 64)
                    ac.wait_ge(zt_done, NTR)
                elif steps[i - 2][0] == "diff":
                    ac.wait_ge(pa_done, i - 1)
                else:
                    ac.wait_ge(pt_done, use_no[("p", i - 2, len(groups(i - 2)) - 1)] + 1)
                for m in range(2):
                    ac.activation(ex[:, b, m * w:(m + 1) * w], s_view(i)[:, m, :], ACT.Exp, bias=soft[:, 16 * b + m:16 * b + m + 1],
                                  scale=SCALE, accum_out=soft[:, 16 * b + 2 + m:16 * b + 3 + m]).then_inc(ex_done, 1)
                if kind == "swa":
                    ac.activation(soft[:, 16 * b + 4:16 * b + 6], soft[:, 16 * b + 10:16 * b + 12], ACT.Exp).then_inc(ex_done, 1)

            exponentials(0)
            exponentials(1)
            for i in range(NSTEP):
                for j, g in enumerate(groups(i)):
                    if j == 0:
                        continue
                    n = use_no[("p", i, j)]
                    ac.wait_ge(pt_done, n + 1)
                    if i >= 2:
                        ac.wait_ge(pv_done, i - 1)
                    w = len(g) * P
                    ac.activation(pt[:, (i % 2) * 1024 + 512:(i % 2) * 1024 + 512 + w], bank(6)[:, 0:w], ACT.Copy).then_inc(pt_act, 1)
                if i + 2 < NSTEP:
                    exponentials(i + 2)
                for q in flush.get(i, []):
                    attention_hi(ac, q)
            for q in flush.get(NSTEP, []):
                attention_hi(ac, q)

            for m in range(12):
                ac.wait_ge(b_tr, m + 1)
                ac.activation(br_v[:, m // 2, (m % 2) * 512:(m % 2) * 512 + 512], bank(5 + m % 2), ACT.Copy).then_inc(b_cp, 1)

            def split_merge(s):
                if s < NS:
                    split_hi(s)

            split_merge(20)
            for s in range(21, 23):
                split_merge(s)
            for m in range(2 * NT):
                ac.wait_ge(mt_done, m + 1)
                i, j = m // 2, m % 2
                ac.activation(ah[:, 4 * j:4 * j + 4, i * P:(i + 1) * P], bank(5 + m % 3).rearrange("p (k n) -> p k n", k=4), ACT.Copy).then_inc(mh_done, 1)
                if m == 0:
                    split_merge(23)
            split_merge(24)
            for n in range(2):
                for i in range(NT):
                    ac.wait_ge(tile_mm, 5 * (23 + 2 * n) + i + 1)
                    if n + i:
                        ac.wait_ge(y_cp, 5 * n + i)
                    link(ac.activation(yr[:, i, n * 512:n * 512 + 512], bank(i), ACT.Copy))
                    ac.activation(osq[:, :], bank(i), ACT.Square, accum_out=stat[:, 48 + 5 * n + i:49 + 5 * n + i]).then_inc(y_cp, 1)
                if n == 0:
                    split_merge(25)
            for i in range(NT):
                ac.wait_ge(x1_done, i + 1)
                if i:
                    ac.wait_ge(x1sq, i)
                ac.activation(pt[:, 1024:2048], xrow[:, i, :], ACT.Square, accum_out=stat[:, 32 + i:33 + i]).then_inc(x1sq, 1)
            for m in range(2 * NT):
                i, j = m // 2, m % 2
                ac.wait_ge(h2t_done, m + 1)
                if m == 0:
                    ac.wait_ge(b_cp, 12)
                if i:
                    ac.wait_ge(rl_done, i)
                ac.activation(h2T[:, j * 512:j * 512 + 512], bank(5 + j), ACT.Copy).then_inc(h2t_cp, 1)
            ac.wait_ge(r_exp_in, 1)
            ac.activation(rex[:, :], rex[:, :], ACT.Exp).then_inc(r_exp, 1)

            def moe_split(r, k, slot, hl, land, used):
                ac.wait_ge(raw_in[slot], land)
                if used is not None:
                    ac.wait_ge(moe_mm, used)
                ac.activation(whi(hl), raw(slot), ACT.Copy).then_inc(hi_done, 1)

            def early(r, ks):
                for k in ks:
                    if r == 0 and k < 3:
                        ac.wait_ge(tile_mm, 5 * (NS + k - HL + 1))
                    moe_split(r, k, k, (2 + k) % 3, 16 * (before[k] + NE * r + 1), None if r == 0 and k < 3 else UPR * r + k - 2)

            def x_high(n, par):
                ac.wait_ge(moe_xt, n + 1)
                ac.activation(act_hi[:, par * D:(par + 1) * D], bank(0, 2), ACT.Copy).then_inc(moe_xh, 1)

            def silu(n, s6):
                ac.wait_ge(moe_mm, s6)
                ac.wait_ge(moe_gp, n)
                ac.activation(gsil[:, :], bank(2), ACT.Silu).then_inc(moe_si, 1)

            def expert(r, e, par, pair, last):
                n = e + NE * r
                s6 = e * 6 + UPR * r
                silu(n, s6)
                if not last:
                    x_high(n + 1, 1 - par)
                splits = [2, 3] if last else [2, 3, 4, 5, 6, 7]
                for j in splits:
                    if (not last and j == 5) or (last and j == 3):
                        ac.wait_ge(moe_gt, n + 1)
                        ac.activation(act_hi[:, 2 * D:2 * D + FE], bank(4), ACT.Copy).then_inc(moe_gh, 1)
                    if j == 7:
                        y_half(n, par, s6, pair, last)
                    slot = (2 + j) % 6
                    moe_split(r, None, slot, (1 + j) % 3, (e + (before[slot] + NE * r + 1 + (2 + j) // 6)) * 16, s6 + j)
                if last:
                    y_half(n, par, s6, pair, last)

            def y_half(n, par, s6, pair, last):
                ac.wait_ge(moe_mm, s6 + (5 if last else 7))
                ac.wait_ge(moe_sc[par], pair * 16)
                ac.activation(ysb[:, par * D:par * D + 512], bank(5), ACT.Copy).then_inc(moe_ya, 1)

            def a_round(r):
                early(r, range(3))
                x_high(NE * r, 0)
                early(r, [3])
                ac.wait_ge(moe_mm, UPR * r + 2)
                with ac.Fori(0, NE // 2 - 1) as i:
                    for j in range(2):
                        expert(r, i * 2 + j, j, i + NE * r // 2, False)
                expert(r, NE - 2, 0, NE // 2 - 1 + NE * r // 2, False)
                expert(r, NE - 1, 1, NE // 2 - 1 + NE * r // 2, True)

            a_round(0)
            ac.wait_ge(tab_done, 1)
            most = ac.value_load(cnt_i[0:1, 0:1], min_val=0, max_val=TOK)
            for r in range(1, ROUNDS):
                with ac.If(most > P * r):
                    a_round(r)

            for m in range(4):
                ac.wait_ge(g2_mm, m + 1)
                if m == 0:
                    ac.wait_ge(all_scattered, 1)
                ac.activation(br_v[:, m // 2, (m % 2) * 512:(m % 2) * 512 + 512], bank(m), ACT.Copy).then_inc(g2_cp, 1)
            for i in range(NT):
                ac.wait_ge(c_sum, i + 1)
                if i:
                    ac.wait_ge(c_sq, i)
                ac.activation(pt[:, 1024:2048], raw_pair(i)[:, 0:D], ACT.Square, accum_out=stat[:, i:i + 1]).then_inc(c_sq, 1)

        @block.tensor
        def _(pe):
            def product(out, k_list, w_hi, w_lo, a_hi, a_lo, first, stop):
                for x, (ka_, kw) in enumerate(k_list):
                    s = first and x == 0
                    e = stop and x == len(k_list) - 1
                    pe.matmul(out, a_hi(ka_), w_hi[:, kw, :], start=s, stop=False)
                    pe.matmul(out, a_hi(ka_), w_lo[:, kw, :], start=False, stop=False)
                    ins = pe.matmul(out, a_lo(ka_), w_hi[:, kw, :], start=False, stop=e)
                return ins

            pe.wait_ge(small_in, 16 * 8)
            pe.wait_ge(const_made, 1)
            pe.transpose(bank(7)[:, 0:97], vecs[0:97, :], ident[0:97, 0:97]).then_inc(v_tr, 1)
            pe.wait_ge(cs_done, 1)
            cs3 = cs[:, :].rearrange("p (k s) -> p k s", s=2)

            def ada(c):
                n = [x for x, u in enumerate(units) if u[:2] == ("ada", c)]
                for x in n:
                    pe.wait_ge(raw_in[x % RAW_MIX], 16 * (x // RAW_MIX + 1))
                for j in range(4):
                    for k in range(KD):
                        col = (4 * c + j) * 2
                        ins = pe.matmul(bank(6)[:, col:col + 2], raw(n[k // 4] % RAW_MIX)[:, k % 4, j * P:(j + 1) * P], cs3[:, k, :],
                                        start=(k == 0), stop=(k == KD - 1))
                ins.then_inc(ada_mm, 1)

            for c in range(4):
                ada(c)
            pe.wait_ge(xn_done, NT)
            for k in range(KD):
                if k >= 2:
                    pe.wait_ge(hf_done, k - 1)
                for i in range(1, NT):
                    pe.transpose(bank(k % 2)[:, (i - 1) * P:i * P], xrow[:, i, k * P:(k + 1) * P], ident[:, :])
                pe.transpose(bank(2 + k % 2)[:, 0:P], xrow[:, 0, k * P:(k + 1) * P], ident[:, :]).then_inc(xt_done, 1)
            pe.wait_ge(cache_in, 16 * 14)
            pe.wait_ge(v_cp, 1)
            for h in range(4):
                pe.transpose(bank(5)[:, h * P:(h + 1) * P], kcache[:, h * P:(h + 1) * P], ident[:, :])
            pe.transpose(bank(7)[:, 0:P], kcache[:, 512:640], ident[:, :]).then_inc(kc_tr, 1)

            tr = 0

            def transpose_rows(c, i):
                nonlocal tr
                if tr < 2:
                    pe.wait_ge(kc_cp, 2)
                else:
                    pe.wait_ge(zt_cp, tr - 1)
                pe.wait_ge(rope_done, tr + 1)
                b = 5 if tr % 2 == 0 else 7
                for h in range(1 if c == 4 else 4):
                    ins = pe.transpose(bank(b)[:, h * P:(h + 1) * P], zr[:, i, h * P:(h + 1) * P], ident[:, :])
                ins.then_inc(zt_done, 1)
                tr += 1

            for c in range(9):
                w = 256 if c == 4 else 512
                for u in range(2):
                    s = 2 * c + u
                    pe.wait_ge(lo_done, s + 1)
                    for i in range(NT):
                        if s == 0 and i == 0:
                            pe.wait_ge(hl_done, KD)
                            pe.wait_ge(hf_done, KD)
                        if u == 0 and c:
                            pe.wait_ge(acc_free, 5 * (c - 1) + i + 1)
                        sl = slice(i * P, (i + 1) * P)
                        product(bank(i)[:, 0:w], [(4 * u + kk, kk) for kk in range(4)], whi(s % HL)[:, :, 0:w], wlo(s % HL)[:, :, 0:w],
                                lambda k: ah[:, k, sl], lambda k: al[:, k, sl], u == 0, u == 1).then_inc(tile_mm, 1)
                        if u == 0 and c - 1 in (0, 1, 3, 4):
                            transpose_rows(c - 1, i)
                if c < 8:
                    ada(4 + c)

            def scores(i, m):
                kind, tile, h, runs, nk, _, _ = steps[i]
                if m == 0:
                    if i >= 2:
                        pe.wait_ge(ex_done, EXC[i - 2])
                    elif i == 0:
                        pe.wait_ge(acc_free, 45)
                        pe.wait_ge(zt_cp, NTR)
                q = (qa_v if kind == "diff" else qb_v)[HD * m:HD * m + HD, h, tile * P:(tile + 1) * P]
                base_ = 3 * (i % 2) * 512
                if kind == "diff":
                    k0, n = runs[0]
                    col = base_ + m * (nk * P if nk > 1 else 512)
                    end, pieces = k0 + n * P, []
                    while k0 < end:
                        w = min(end - k0, 512 - col % 512)
                        pieces.append((col, k0, w))
                        col, k0 = col + w, k0 + w
                    for x, (col, k0, w) in enumerate(pieces if m == 0 else pieces[::-1]):
                        if m == 1 and x == 1:
                            pe.wait_ge(s_half, i + 1)
                        ins = pe.matmul(psum[:, col:col + w], q, ka_v[HD * m:HD * m + HD, h, k0:k0 + w], start=True, stop=True)
                else:
                    col = base_ + m * 512
                    for k0, n in runs:
                        masks = []
                        if k0 >= 2 * P:
                            first = (k0 - 2 * P) // P
                            masks = [(j, mk) for j, mk in ((tile - 2, maskL), (tile, maskR)) if first <= j < first + n]
                        ins = pe.matmul(psum[:, col:col + n * P], q, kbT[HD * m:HD * m + HD, k0:k0 + n * P], start=True, stop=not masks)
                        for x, (j, mk) in enumerate(masks):
                            a = col + (j - first) * P
                            ins = pe.matmul(psum[:, a:a + P], ident16[:, :], mk[:, :], start=False, stop=(x == len(masks) - 1))
                        col += n * P
                ins.then_inc(s_half if m == 0 else s_done, 1)

            prev = [None]

            def turn(n):
                if n:
                    wait_emptied(pe, n - 1)

            scores(0, 0)
            scores(0, 1)
            scores(1, 0)
            scores(1, 1)
            for i in range(NSTEP):
                kind, tile, h, _, nk, vt, q = steps[i]
                b = i % 2
                w = nk * P
                for j, g in enumerate(groups(i)):
                    n = use_no[("p", i, j)]
                    if j == 0:
                        pe.wait_ge(pa_done, i + 1)
                    turn(n)
                    src = ax[:, b, :] if kind == "diff" else ex[:, b, :]
                    for x, kt in enumerate(g):
                        ins = pe.transpose(bank(6)[:, x * P:(x + 1) * P], src[:, kt * P:(kt + 1) * P], ident[:, :])
                    ins.then_inc(pt_done, 1)
                    if i + 2 < NSTEP:
                        scores(i + 2, j)
                if len(groups(i)) == 1 and i + 2 < NSTEP:
                    scores(i + 2, 1)
                for j in range(len(groups(i))):
                    wait_emptied(pe, use_no[("p", i, j)])
                if i == 0 or steps[i - 1][6] != q:
                    pe.wait_ge(o_cp, q)
                ptb = pt[:, b * 1024:(b + 1) * 1024]
                if kind == "diff":
                    for kt in range(nk):
                        ins = pe.matmul(bank(7)[:, h * P:(h + 1) * P], ptb[:, kt * P:(kt + 1) * P], va_v[:, vt[kt], h * P:(h + 1) * P],
                                        start=(kt == 0), stop=(kt == nk - 1))
                else:
                    for n in range(2):
                        for kt in range(nk):
                            x = n * nk + kt
                            ins = pe.matmul(bank(7)[:, n * 256 + h * HD:n * 256 + (h + 1) * HD], ptb[:, x * P:(x + 1) * P],
                                            vb_v[:, vt[kt], n * HD:(n + 1) * HD], start=(kt == 0), stop=(kt == nk - 1))
                ins.then_inc(pv_done, 1)
                for q_ in flush.get(i, []):
                    out_transpose(pe, q_)
            for q_ in flush.get(NSTEP, []):
                out_transpose(pe, q_)

            pe.wait_ge(mod_done, 2)
            wait_emptied(pe, len(uses) - 1)
            for m in range(12):
                if m >= 2:
                    pe.wait_ge(b_cp, m - 1)
                for x in range(4):
                    col = (m // 2) * 8 + (m % 2) * 4 + x
                    ins = pe.matmul(bank(5 + m % 2)[:, x * P:(x + 1) * P], modr[:, col:col + 1].broadcast_to([P, P]), ident[:, :], start=True, stop=True)
                ins.then_inc(b_tr, 1)

            for g in range(4):
                s = 18 + g
                pe.wait_ge(lo_done, s + 1)
                for i in range(NT):
                    if g:
                        pe.wait_ge(mix_done, 5 * (g - 1) + i + 1)
                    q = [0, 2, 3, 4, 5][i] if g % 2 == 0 else [1, 6, 7, 8, 9][i]
                    pe.wait_ge(ol_done, q + 1)
                    pe.wait_ge(oh_done, q + 1)
                    sl = slice(i * P, (i + 1) * P)
                    product(bank(i), [(4 * (g % 2) + kk, kk) for kk in range(4)], whi(s % HL), wlo(s % HL),
                            lambda k: ah[:, k, sl], lambda k: al[:, k, sl], True, True).then_inc(tile_mm, 1)
            for m in range(2 * NT):
                i, j = m // 2, m % 2
                pe.wait_ge(mix_done, 15 + i + 1)
                if m < 3:
                    pe.wait_ge(b_cp, 12)
                    pe.wait_ge(o_cp, NOUT)
                else:
                    pe.wait_ge(mh_done, m - 2)
                    pe.wait_ge(ml_done, m - 2)
                for x in range(4):
                    k = 4 * j + x
                    ins = pe.transpose(bank(5 + m % 3)[:, x * P:(x + 1) * P], xrow[:, i, k * P:(k + 1) * P], ident[:, :])
                ins.then_inc(mt_done, 1)
            for n in range(2):
                for u in range(2):
                    s = 22 + 2 * n + u
                    pe.wait_ge(lo_done, s + 1)
                    for i in range(NT):
                        if n == 0 and u == 0:
                            pe.wait_ge(mh_done, 2 * i + 2)
                            pe.wait_ge(ml_done, 2 * i + 2)
                        if n == 1 and u == 0:
                            pe.wait_ge(y_cp, i + 1)
                        sl = slice(i * P, (i + 1) * P)
                        product(bank(i), [(4 * u + kk, kk) for kk in range(4)], whi(s % HL), wlo(s % HL),
                                lambda k: ah[:, k, sl], lambda k: al[:, k, sl], u == 0, u == 1).then_inc(tile_mm, 1)
            for m in range(2 * NT):
                i, j = m // 2, m % 2
                pe.wait_ge(h2_done, i + 1)
                if m >= 2:
                    pe.wait_ge(h2t_cp, m - 1)
                for x in range(4):
                    k = 4 * j + x
                    ins = pe.transpose(bank(5 + j)[:, x * P:(x + 1) * P], yr[:, i, k * P:(k + 1) * P], ident[:, :])
                ins.then_inc(h2t_done, 1)
                if j == 1:
                    pe.wait_ge(h2t_cp, m + 1)
                    for k in range(KD):
                        ins = pe.matmul(bank(7)[:, i * NR:(i + 1) * NR], h2T[:, k * P:(k + 1) * P], wr_v[:, k, :], start=(k == 0), stop=(k == KD - 1))
                    ins.then_inc(rl_done, 1)
            pe.wait_ge(m_ready, 1)
            m3 = m16[:, :].rearrange("p (t e) -> p t e", t=NT)
            for i in range(NT):
                for a in range(i):
                    pe.matmul(bank(5)[:, i * NE:(i + 1) * NE], ones16[:, :], m3[:, a, :], start=(a == 0), stop=False)
                pe.matmul(bank(5)[:, i * NE:(i + 1) * NE], upper16[:, :], m3[:, i, :], start=(i == 0), stop=True)
            for a in range(NT):
                ins = pe.matmul(bank(5)[:, NT * NE:(NT + 1) * NE], ones16[:, :], m3[:, a, :], start=(a == 0), stop=(a == NT - 1))
            ins.then_inc(pre_done, 1)
            for x in range(2 * NT):
                pe.wait_ge(oc_done, x + 1)
                i, k = x // 2, x % 2
                ins = pe.matmul(bank(6)[:, 0:ROUNDS * NE], roc[:, (x % 2) * P:(x % 2 + 1) * P], rrhs[k][:, i * ROUNDS * NE:(i + 1) * ROUNDS * NE],
                                start=(x == 0), stop=(x == 2 * NT - 1))
                ins.then_inc(tab_mm, 1)

            def transpose_x(n, par, pair):
                pe.wait_ge(moe_g[par], pair * 16 + 16)
                pe.wait_ge(moe_xh, n)
                pe.wait_ge(moe_xl, n)
                for k in range(KD):
                    ins = pe.transpose(bank(k // 4)[:, (k % 4) * P:(k % 4 + 1) * P], xg[:, par * D + k * P:par * D + (k + 1) * P], ident[:, :])
                ins.then_inc(moe_xt, 1)

            def unit(ready, hl, out, k_list, off, first, stop, signal):
                pe.wait_ge(lo_done, ready)
                product(out, k_list, whi(hl), wlo(hl), lambda k: act_hi[:, off + k * P:off + (k + 1) * P],
                        lambda k: act_lo[:, off + k * P:off + (k + 1) * P], first, stop).then_inc(moe_mm, 1)

            def up(ready, hl, b_, par, u):
                unit(ready, hl, bank(b_), [(4 * u + kk, kk) for kk in range(4)], par * D, u == 0, u == 1, None)

            def expert(r, e, par, pair, last):
                n = e + NE * r
                s = e * 6 + (NS + UPR * r + 2)
                if not last:
                    transpose_x(n + 1, 1 - par, pair + par)
                pe.wait_ge(moe_gp, n)
                up(s + 1, 1, 3, par, 0)
                up(s + 2, 2, 3, par, 1)
                j = 2
                if not last:
                    pe.wait_ge(moe_si, n + 1)
                    pe.wait_ge(moe_xl, n + 2)
                    pe.wait_ge(moe_xh, n + 2)
                    up(s + 3, 0, 2, 1 - par, 0)
                    j = 4
                pe.wait_ge(moe_gp, n + 1)
                pe.wait_ge(moe_gl, n)
                for x in range(4):
                    ins = pe.transpose(bank(4)[:, x * P:(x + 1) * P], gprod[:, x * P:(x + 1) * P], ident[:, :])
                ins.then_inc(moe_gt, 1)
                if not last:
                    up(s + 4, 1, 2, 1 - par, 1)
                pe.wait_ge(moe_gl, n + 1)
                pe.wait_ge(moe_gh, n + 1)
                pe.wait_ge(moe_ya, n)
                unit(s + j + 1, (1 + j) % 3, bank(5), [(kk, kk) for kk in range(4)], 2 * D, True, True, None)
                pe.wait_ge(moe_yv, n)
                unit(s + j + 2, (2 + j) % 3, bank(6), [(kk, kk) for kk in range(4)], 2 * D, True, True, None)

            def a_round(r):
                transpose_x(NE * r, 0, NE * r // 2)
                pe.wait_ge(moe_xl, NE * r + 1)
                pe.wait_ge(moe_xh, NE * r + 1)
                pe.wait_ge(moe_si, NE * r)
                up(NS + UPR * r + 1, 2, 2, 0, 0)
                up(NS + UPR * r + 2, 0, 2, 0, 1)
                with pe.Fori(0, NE // 2 - 1) as i:
                    for j in range(2):
                        expert(r, i * 2 + j, j, i + NE * r // 2, False)
                expert(r, NE - 2, 0, NE // 2 - 1 + NE * r // 2, False)
                expert(r, NE - 1, 1, NE // 2 - 1 + NE * r // 2, True)

            pe.wait_ge(y_cp, 10)
            pe.wait_ge(tab_done, 1)
            a_round(0)
            most = pe.value_load(cnt_i[0:1, 0:1], min_val=0, max_val=TOK)
            for r in range(1, ROUNDS):
                with pe.If(most > P * r):
                    a_round(r)

            pe.wait_ge(all_scattered, 1)
            for m in range(4):
                for x in range(4):
                    col = 48 + (m // 2) * 8 + (m % 2) * 4 + x
                    ins = pe.matmul(bank(m)[:, x * P:(x + 1) * P], modr[:, col:col + 1].broadcast_to([P, P]), ident[:, :], start=True, stop=True)
                ins.then_inc(g2_mm, 1)

        @block.vector
        def _(ve):
            chain = [0]

            def link(ins):
                chain[0] += 1
                ins.then_inc(ve_link, 1)
                ve.wait_ge(ve_link, chain[0])

            def split_lo(s):
                n = unit_of_split[s]
                _, w = unit_src(n)
                ve.wait_ge(hi_done, s + 1)
                ve.tensor_tensor(wlo(s % HL)[:, :, 0:w], raw(n % RAW_MIX)[:, :, 0:w], whi(s % HL)[:, :, 0:w].bitcast(F32), ALU.subtract).then_inc(lo_done, 1)

            ve.wait_ge(v_tr, 1)
            ve.tensor_copy(vT[:, 0:97], bank(7)[:, 0:97]).then_inc(v_cp, 1)
            ve.wait_ge(v_cp, 1)
            ve.tensor_scalar(gh[:, 0:1], vT[:, 96:97], 1.0 - LAMBDA_INIT, None, ALU.mult)
            mc = modc[:, :].rearrange("p (j s) -> p j s", s=2)
            mx4 = modx[:, :].rearrange("p (a k s) -> p a k s", a=2, k=KD)
            ve.wait_ge(ada_mm, 4)
            pm = bank(6)[:, 0:96].rearrange("p (j s) -> p j s", s=2)
            link(ve.tensor_tensor(mc[:, 0:16, :], pm[:, 0:16, :], vT[:, 16:32].unsqueeze(2).broadcast_to([P, 16, 2]), ALU.add))
            link(ve.tensor_scalar(mx4[:, 0], mc[:, 8:16, :], 1.0, None, ALU.add))
            link(ve.tensor_tensor(mx4[:, 0], mx4[:, 0], vT[:, 64:72].unsqueeze(2).broadcast_to([P, 8, 2]), ALU.mult))
            split_lo(0)
            split_lo(1)
            for k in range(KD):
                ve.wait_ge(xt_done, k + 1)
                if k >= 2:
                    ve.wait_ge(hh_done, k - 1)
                f = hf[:, (k % 2) * TOK:(k % 2 + 1) * TOK]
                link(ve.tensor_scalar(f[:, P:TOK], bank(k % 2), mx4[:, 0, k, 1:2], mc[:, k, 1:2], ALU.mult, ALU.add))
                ve.tensor_scalar(f[:, 0:P], bank(2 + k % 2)[:, 0:P], mx4[:, 0, k, 0:1], mc[:, k, 0:1], ALU.mult, ALU.add).then_inc(hf_done, 1)
                ve.wait_ge(hh_done, k + 1)
                ve.tensor_tensor(al[:, k, :], f, ah[:, k, :].bitcast(F32), ALU.subtract).then_inc(hl_done, 1)

            rope_no = [0]

            def rope(c, i):
                n_ = rope_no[0]
                k = {0: 0, 1: 1, 3: 2, 4: 3}[c]
                ve.wait_ge(acc_free, 5 * c + i + 1)
                if k:
                    ve.wait_ge(zt_done, 5 * (k - 1) + i + 1)
                w = P if c == 4 else 512
                nh = w // HD
                z, o = zs[:, i, 0:w], zr[:, i, 0:w]
                if c == 3:
                    z = z.rearrange("p (n g d) -> p n g d", n=2, g=4)
                    o = o.rearrange("p (g n d) -> p n g d", g=4, n=2)
                if i == 0:
                    ve.tensor_copy(o, z).then_inc(rope_done, 1)
                    return
                C = cs_v[:, i - 1, 0, :]
                if c == 3:
                    for n in range(2):
                        link(ve.tensor_tensor(o[:, n], z[:, n], C.unsqueeze(1).broadcast_to([P, 4, HD]), ALU.mult))
                else:
                    link(ve.tensor_tensor(o.rearrange("p (h d) -> p h d", h=nh), z.rearrange("p (h d) -> p h d", h=nh),
                                          C.unsqueeze(1).broadcast_to([P, nh, HD]), ALU.mult))
                ve.wait_ge(rope_b, n_ + 1)
                of_ = zr[:, i, 0:w]
                ve.tensor_tensor(of_, of_, rt[:, n_ % 2, 0:w], ALU.add).then_inc(rope_done, 1)
                rope_no[0] += 1

            for c in range(9):
                split_lo(2 * c + 2)
                if c in (0, 1, 3, 4):
                    for i in range(NT):
                        rope(c, i)
                split_lo(2 * c + 3)

            ve.wait_ge(ada_mm, 12)
            link(ve.tensor_tensor(mc[:, 16:48, :], pm[:, 16:48, :], vT[:, 32:64].unsqueeze(2).broadcast_to([P, 32, 2]), ALU.add))
            mr = modr[:, :].rearrange("p (a s k) -> p a k s", a=4, s=2)

            def g8(c0):
                return vT[:, c0:c0 + 8].unsqueeze(2).broadcast_to([P, 8, 2])

            link(ve.tensor_tensor(mr[:, 0], mc[:, 16:24, :], g8(72), ALU.mult))
            link(ve.tensor_scalar(mr[:, 1], mc[:, 32:40, :], 1.0, None, ALU.add))
            link(ve.tensor_tensor(mr[:, 1], mr[:, 1], g8(80), ALU.mult))
            link(ve.tensor_copy(mr[:, 2], mc[:, 24:32, :]))
            ve.tensor_tensor(mr[:, 3], mc[:, 40:48, :], g8(88), ALU.mult).then_inc(mod_done, 2)

            ve.wait_ge(cache_in, 16 * 14)
            for x in range(2):
                ve.tensor_tensor_reduce(osq[:, x * HD:(x + 1) * HD], lam[:, 2 * x * HD:(2 * x + 1) * HD], lam[:, (2 * x + 1) * HD:(2 * x + 2) * HD],
                                        1.0, 0.0, ALU.mult, ALU.add, lamv[:, x:x + 1]).then_inc(lam_part, 1)
            ve.wait_ge(lam_part, 2)
            ve.tensor_scalar(nsink[:, :], sinkb[:, :], -1.0, None, ALU.mult).then_inc(lam_sum, 1)
            ve.wait_ge(lam_exp, 1)
            link(ve.tensor_tensor(lamv[:, 4:5], lamv[:, 3:4], lamv[:, 2:3], ALU.subtract))
            link(ve.tensor_scalar(lamv[:, 4:5], lamv[:, 4:5], -LAMBDA_INIT, None, ALU.add))

            def maximum(i):
                kind, b = steps[i][0], i % 2
                so = soft[:, 16 * b:16 * b + 16]
                ve.wait_ge(s_done, i + 1)
                link(ve.reduce_max(so[:, 8:10], s_view(i), AX.X))
                if kind == "diff":
                    ve.tensor_scalar(so[:, 0:2], so[:, 8:10], -SCALE, None, ALU.mult).then_inc(mx_done, 1)
                else:
                    g = steps[i][2]
                    ns = nsink[:, :].rearrange("p (n g) -> p n g", n=2)[:, :, g]
                    link(ve.scalar_tensor_tensor(so[:, 0:2], so[:, 8:10], -SCALE, ns, ALU.mult, ALU.min))
                    ve.tensor_tensor(so[:, 10:12], so[:, 0:2], ns, ALU.subtract).then_inc(mx_done, 1)

            def combine(i):
                kind, b, w = steps[i][0], i % 2, steps[i][4] * P
                so = soft[:, 16 * b:16 * b + 16]
                ve.wait_ge(ex_done, EXC[i])
                if kind == "diff":
                    link(ve.reciprocal(so[:, 6:8], so[:, 2:4]))
                    link(ve.tensor_tensor(so[:, 7:8], so[:, 7:8], lamv[:, 4:5], ALU.mult))
                    if i >= 2:
                        ve.wait_ge(pt_done, use_no[("p", i - 2, len(groups(i - 2)) - 1)] + 1)
                    link(ve.tensor_scalar(ax[:, b, 0:w], ex[:, b, 0:w], so[:, 6:7], None, ALU.mult))
                    ve.scalar_tensor_tensor(ax[:, b, 0:w], ex[:, b, w:2 * w], so[:, 7:8], ax[:, b, 0:w], ALU.mult, ALU.add).then_inc(pa_done, 1)
                else:
                    g, q = steps[i][2], steps[i][6]
                    link(ve.tensor_tensor(so[:, 2:4], so[:, 2:4], so[:, 4:6], ALU.add))
                    r8 = rr[:, 8 * (q % 2):8 * (q % 2) + 8].rearrange("p (n g) -> p n g", n=2)[:, :, g]
                    ve.reciprocal(r8, so[:, 2:4]).then_inc(pa_done, 1)

            def output(q):
                i = last_step[q]
                ve.wait_ge(pv_done, i + 1)
                if q:
                    ve.wait_ge(pt_done, use_no[("o", q - 1, 0)] + 1)
                if steps[i][0] == "diff":
                    ve.tensor_copy(orow[:, :], bank(7)).then_inc(o_cp, 1)
                    ve.wait_ge(o_cp, q + 1)
                    for h in range(AH):
                        a = orow[:, h * AV:(h + 1) * AV]
                        ve.tensor_tensor_reduce(osq[:, h * AV:(h + 1) * AV], a, a, 1.0, 0.0, ALU.mult, ALU.add, stat[:, 16 + h:17 + h]).then_inc(head_sum, 1)
                else:
                    ve.wait_ge(pa_done, i + 1)
                    o3 = orow[:, :].rearrange("p (h d) -> p h d", h=BH)
                    ve.tensor_tensor(o3, bank(7).rearrange("p (h d) -> p h d", h=BH),
                                     rr[:, 8 * (q % 2):8 * (q % 2) + 8].unsqueeze(2).broadcast_to([P, BH, HD]), ALU.mult).then_inc(o_cp, 1)

            maximum(0)
            maximum(1)
            combine(0)
            for i in range(NSTEP):
                g = groups(i)[0]
                ve.wait_ge(pt_done, use_no[("p", i, 0)] + 1)
                if i >= 2:
                    ve.wait_ge(pv_done, i - 1)
                w = len(g) * P
                ve.tensor_copy(pt[:, (i % 2) * 1024:(i % 2) * 1024 + w], bank(6)[:, 0:w]).then_inc(pt_dve, 1)
                for q in range(NOUT):
                    if last_step[q] == i - 1:
                        output(q)
                if i + 1 < NSTEP:
                    combine(i + 1)
                if i + 2 < NSTEP:
                    maximum(i + 2)
                for q in flush.get(i, []):
                    attention_lo(ve, q)
            output(NOUT - 1)
            for q in flush.get(NSTEP, []):
                attention_lo(ve, q)

            split_lo(20)
            for g in range(4):
                for i in range(NT):
                    m, n = 5 * g + i, g // 2
                    ve.wait_ge(tile_mm, 5 * (18 + g) + i + 1)
                    ve.wait_ge(g_in[m % 2], 16 * (m // 2 + 1))
                    if m == 0:
                        ve.wait_ge(oh_done, NOUT)
                    dst = xrow[:, i, n * 512:n * 512 + 512]
                    if g % 2 == 0:
                        ve.tensor_tensor(dst, bank(i), gst[:, m % 2, :], ALU.mult).then_inc(mix_done, 1)
                    else:
                        ve.wait_ge(mix_done, m)
                        link(ve.tensor_tensor(mtmp, bank(i), gst[:, m % 2, :], ALU.mult))
                        ve.tensor_tensor(dst, dst, mtmp, ALU.add).then_inc(mix_done, 1)
                if g < 2:
                    split_lo(21 + g)
            for m in range(2 * NT):
                i, j = m // 2, m % 2
                ve.wait_ge(mh_done, m + 1)
                d = (slice(None), slice(4 * j, 4 * j + 4), slice(i * P, (i + 1) * P))
                ve.tensor_tensor(al[d], bank(5 + m % 3).rearrange("p (k n) -> p k n", k=4), ah[d].bitcast(F32), ALU.subtract).then_inc(ml_done, 1)
                if m == 0:
                    split_lo(23)
            split_lo(24)
            split_lo(25)
            ve.wait_ge(y_cp, 10)
            ve.tensor_tensor(stat[:, 0:5], stat[:, 48:53], stat[:, 53:58], ALU.add).then_inc(ysum, 1)
            ve.wait_ge(yrs, 1)
            ve.wait_ge(b_cp, 12)
            for i in range(NT):
                ve.scalar_tensor_tensor(yr[:, i, :], yr[:, i, :], stat[:, 8 + i:9 + i], br_v[:, min(i, 1), :], ALU.mult, ALU.mult).then_inc(yn, 1)
            ve.wait_ge(x1rs, 1)
            for i in range(NT):
                link(ve.scalar_tensor_tensor(yr[:, i, :], xrow[:, i, :], stat[:, 40 + i:41 + i], br_v[:, 2 + min(i, 1), :], ALU.mult, ALU.mult))
                ve.tensor_tensor(yr[:, i, :], yr[:, i, :], br_v[:, 4 + min(i, 1), :], ALU.add).then_inc(h2_done, 1)

            ve.wait_ge(rl_done, NT)
            L = rL[:, :].rearrange("p (t n) -> p t n", t=NT)
            link(ve.tensor_tensor(L, bank(7)[:, 0:NT * NR].rearrange("p (t n) -> p t n", t=NT), br[:, :].unsqueeze(1).broadcast_to([P, NT, NR]), ALU.add))

            def s5(x):
                return rsm[:, x * NT:(x + 1) * NT]

            def wide(a, n):
                return a.unsqueeze(2).broadcast_to([P, NT, n])

            E3 = rex[:, :].rearrange("p (t n) -> p t n", t=NT)
            T1 = rt1[:, :].rearrange("p (t n) -> p t n", t=NT)
            T2 = rt2[:, :].rearrange("p (t n) -> p t n", t=NT)
            LE = rle[:, :].rearrange("p (t n) -> p t n", t=NT)
            OH = [o[:, :].rearrange("p (t n) -> p t n", t=NT) for o in oh]
            io = iota32[:, :].unsqueeze(1).broadcast_to([P, NT, NE])

            def first_of(onehot, vals, best, n, at_):
                link(ve.tensor_tensor(T1[:, :, 0:n], vals, wide(best, n), ALU.not_equal))
                link(ve.scalar_tensor_tensor(T1[:, :, 0:n], T1[:, :, 0:n], 64.0, io[:, :, 0:n], ALU.mult, ALU.add))
                link(ve.tensor_reduce(at_, T1[:, :, 0:n], AX.X, ALU.min))
                link(ve.tensor_tensor(onehot, io[:, :, 0:n], wide(at_, n), ALU.is_equal))

            link(ve.reduce_max(s5(0), L[:, :, 0:NG], AX.X))
            link(ve.tensor_tensor(E3[:, :, 0:NG], L[:, :, 0:NG], wide(s5(0), NG), ALU.subtract))
            first_of(T2[:, :, 0:NG], L[:, :, 0:NG], s5(0), NG, s5(1))
            link(ve.tensor_scalar(T2[:, :, 0:NG], T2[:, :, 0:NG], 1.0, -NEG, ALU.subtract, ALU.mult))
            for i in range(NT):
                link(ve.tensor_tensor(LE[:, i, :].rearrange("p (g e) -> p g e", g=NG), L[:, i, NG:NR].rearrange("p (g e) -> p g e", g=NG),
                                      T2[:, i, 0:NG].unsqueeze(2).broadcast_to([P, NG, EPG]), ALU.add))
            link(ve.reduce_max(s5(2), LE, AX.X))
            first_of(OH[0], LE, s5(2), NE, s5(3))
            link(ve.scalar_tensor_tensor(LE, OH[0], 2 * NEG, LE, ALU.mult, ALU.add))
            link(ve.reduce_max(s5(4), LE, AX.X))
            first_of(OH[1], LE, s5(4), NE, s5(5))
            link(ve.tensor_tensor(m16[:, :], oh[0][:, :], oh[1][:, :], ALU.add))
            ve.tensor_tensor(E3[:, :, 4:5], s5(4).unsqueeze(2), s5(2).unsqueeze(2), ALU.subtract).then_inc(r_exp_in, 1)
            ve.wait_ge(r_exp_in, 1)
            ve.sem_inc(m_ready, 1)
            ve.wait_ge(r_exp, 1)
            link(ve.tensor_reduce(s5(6), E3[:, :, 0:NG], AX.X, ALU.add))
            link(ve.tensor_scalar(s5(7), E3[:, :, 4], 1.0, None, ALU.add))
            link(ve.tensor_tensor(s5(6), s5(6), s5(7), ALU.mult))
            link(ve.reciprocal(wk[:, 0:NT], s5(6)))
            link(ve.tensor_tensor(wk[:, NT:2 * NT], wk[:, 0:NT], E3[:, :, 4], ALU.mult))
            ve.wait_ge(pre_done, 1)
            link(ve.tensor_copy(rpre[:, :], bank(5)[:, 0:NT * NE]))
            link(ve.tensor_reduce(s5(8)[:, 0:1], bank(5)[:, NT * NE:(NT + 1) * NE], AX.X, ALU.max))
            link(ve.tensor_copy(cnt_i[:, 0:1], s5(8)[:, 0:1]))
            PR = rpre[:, :].rearrange("p (t n) -> p t n", t=NT)
            for k in range(2):
                pos, rnd = rposk[:, k * NT:(k + 1) * NT], rround[:, k * NT:(k + 1) * NT]
                link(ve.tensor_tensor(T1, OH[k], PR, ALU.mult))
                link(ve.tensor_reduce(pos, T1, AX.X, ALU.add))
                link(ve.tensor_scalar(rnd, pos, float(P), None, ALU.is_ge))
                for x in range(2, ROUNDS):
                    link(ve.scalar_tensor_tensor(rnd, pos, float(P * x), rnd, ALU.is_ge, ALU.add))
                link(ve.scalar_tensor_tensor(pos, rnd, -float(P), pos, ALU.mult, ALU.add))
                tv = tokval[:, :].rearrange("p (t k) -> p t k", k=2)[:, :, k]
                R4 = rrhs[k][:, :].rearrange("p (t r n) -> p t r n", t=NT, r=ROUNDS)
                for x in range(ROUNDS):
                    link(ve.scalar_tensor_tensor(s5(9), rnd, float(x), tv, ALU.is_equal, ALU.mult))
                    link(ve.tensor_tensor(R4[:, :, x, :], OH[k], wide(s5(9), NE), ALU.mult))
            for x in range(2 * NT):
                i, k = x // 2, x % 2
                if x >= 2:
                    ve.wait_ge(tab_mm, x - 1)
                ve.tensor_scalar(roc[:, (x % 2) * P:(x % 2 + 1) * P], cidx[:, :], rposk[:, k * NT + i:k * NT + i + 1], None, ALU.is_equal).then_inc(oc_done, 1)
            ve.wait_ge(tab_mm, 2 * NT)
            tab_i = rt1[:, 0:ROUNDS * NE].bitcast(I32)
            link(ve.tensor_scalar(tab_i, bank(6)[:, 0:ROUNDS * NE], -1.0, None, ALU.add))
            link(ve.tensor_copy(tab_s[:, :], tab_i.bitcast(U32)))
            ve.tensor_scalar(tab_g[:, :], tab_s[:, :], 1, None, ALU.logical_shift_right).then_inc(tab_done, 1)

            def moe_lo(ready, slot, hl):
                ve.wait_ge(hi_done, ready)
                ve.tensor_tensor(wlo(hl), raw(slot), whi(hl).bitcast(F32), ALU.subtract).then_inc(lo_done, 1)

            def x_low(n, par):
                ve.wait_ge(moe_xh, n + 1)
                ve.tensor_tensor(act_lo[:, par * D:(par + 1) * D], bank(0, 2), act_hi[:, par * D:(par + 1) * D].bitcast(F32), ALU.subtract).then_inc(moe_xl, 1)

            def expert(r, e, par, pair, last):
                n = e + NE * r
                s = e * 6 + (NS + UPR * r + 2)
                if not last:
                    x_low(n + 1, 1 - par)
                for j in ([2, 3] if last else [2, 3, 4, 5, 6, 7]):
                    if (not last and j == 4) or (last and j == 2):
                        ve.wait_ge(moe_mm, e * 6 + (UPR * r + 4))
                        ve.wait_ge(moe_si, n + 1)
                        ve.wait_ge(moe_gt, n)
                        ve.tensor_tensor(gprod[:, :], bank(3), gsil[:, :], ALU.mult).then_inc(moe_gp, 1)
                    if (not last and j == 5) or (last and j == 3):
                        ve.wait_ge(moe_gh, n + 1)
                        ve.tensor_tensor(act_lo[:, 2 * D:2 * D + FE], bank(4), act_hi[:, 2 * D:2 * D + FE].bitcast(F32), ALU.subtract).then_inc(moe_gl, 1)
                    moe_lo(s + j + 1, (2 + j) % 6, (1 + j) % 3)
                ve.wait_ge(moe_mm, e * 6 + (UPR * r + (6 if last else 8)))
                ve.wait_ge(moe_sc[par], pair * 16)
                ve.tensor_copy(ysb[:, par * D + 512:(par + 1) * D], bank(6)).then_inc(moe_yv, 1)

            def a_round(r):
                for k in range(3):
                    moe_lo(NS + UPR * r + k + 1, k, (2 + k) % 3)
                x_low(NE * r, 0)
                moe_lo(NS + UPR * r + 4, 3, 2)
                with ve.Fori(0, NE // 2 - 1) as i:
                    for j in range(2):
                        expert(r, i * 2 + j, j, i + NE * r // 2, False)
                expert(r, NE - 2, 0, NE // 2 - 1 + NE * r // 2, False)
                expert(r, NE - 1, 1, NE // 2 - 1 + NE * r // 2, True)

            a_round(0)
            most = ve.value_load(cnt_i[0:1, 0:1], min_val=0, max_val=TOK)
            for r in range(1, ROUNDS):
                with ve.If(most > P * r):
                    a_round(r)

            for i in range(NT):
                ve.wait_ge(yp_in[i], 16)
                y2 = raw_pair(i)
                ve.tensor_scalar(y2[:, 0:D], y2[:, 0:D], wk[:, i:i + 1], None, ALU.mult).then_inc(c_part, 1)
                ve.wait_ge(c_part, i + 1)
                ve.scalar_tensor_tensor(y2[:, 0:D], y2[:, D:2 * D], wk[:, NT + i:NT + i + 1], y2[:, 0:D], ALU.mult, ALU.add).then_inc(c_sum, 1)
            ve.wait_ge(c_rs, 1)
            ve.wait_ge(g2_cp, 4)
            for i in range(NT):
                y2 = raw_pair(i)
                ve.scalar_tensor_tensor(y2[:, 0:D], y2[:, 0:D], stat[:, 8 + i:9 + i], br_v[:, min(i, 1), :], ALU.mult, ALU.mult).then_inc(c_part, 1)
                ve.wait_ge(c_part, NT + i + 1)
                ve.tensor_tensor(xrow[:, i, :], xrow[:, i, :], y2[:, 0:D], ALU.add).then_inc(c_out, 1)


_INS = ['x_prompt', 'x_sample', 'c', 'cache_diff_k', 'cache_diff_v', 'cache_swa_k', 'cache_swa_v', 'c_ctx',
        'w_ada', 'b_ada', 'g_pre_mix', 'g_post_mix', 'g_pre_ffn', 'g_post_ffn', 'w_in',
        'lam_q1', 'lam_k1', 'lam_q2', 'lam_k2', 'g_diff_head', 'sink', 'w_proj_a', 'w_proj_b', 'w_out',
        'w_router_group', 'b_router_group', 'w_router_expert', 'b_router_expert', 'w_e1', 'w_e3', 'w_e2']
_OUTS = [("y_prompt", (1, CTX, D)), ("y_sample", (1, LAT, D)), ("new_diff_k", (1, 1, CTX, AH, 2, HD)),
         ("new_diff_v", (1, 1, CTX, AH, AV)), ("new_swa_k", (1, 1, CTX, BKV, HD)), ("new_swa_v", (1, 1, CTX, BKV, HD))]


def rope_table():
    grid_w, quarter = 64, HD // 4
    tok = np.arange(LAT)
    inv = (np.float32(10000.0) ** (-np.arange(quarter, dtype=np.float32) / np.float32(quarter))).astype(np.float32)
    ang = np.concatenate([(tok // grid_w).astype(np.float32)[:, None] * inv, (tok % grid_w).astype(np.float32)[:, None] * inv], axis=-1)
    c, s = np.cos(ang), np.sin(ang)
    both = np.stack([np.concatenate([c, c], -1), np.concatenate([-s, s], -1)], 1).astype(np.float32)
    return np.ascontiguousarray(both.reshape(NLT, P, 2 * HD).transpose(1, 0, 2).reshape(P, NLT * 2 * HD))


def kernel(**inputs):
    import concourse.bacc as bacc
    from concourse.bass_utils import run_bass_kernel_spmd

    nc = bacc.Bacc("TRN2", target_bir_lowering=False, num_devices=1)
    arrays, t = {}, {}
    for name in _INS:
        a = np.ascontiguousarray(inputs[name])
        arrays["in_" + name] = a
        t[name] = nc.dram_tensor("in_" + name, a.shape, mybir.dt.from_np(a.dtype), kind="ExternalInput").ap()
    arrays["in_rope"] = rope_table()
    t["rope"] = nc.dram_tensor("in_rope", arrays["in_rope"].shape, F32, kind="ExternalInput").ap()
    for name, shape in _OUTS:
        t[name] = nc.dram_tensor("out_" + name, shape, F32, kind="ExternalOutput").ap()
    build(nc, t)
    r = run_bass_kernel_spmd(nc, [arrays], core_ids=[0])
    return tuple(r.results[0]["out_" + name] for name, _ in _OUTS)
```
